# Optimizing a Trainium2 kernel written in Bass

```python
import jax, jax.numpy as jnp
from jax import lax
import numpy as np
import math

D_MODEL = 1024
BATCH = 1
SEQ = 512
DEPTH = 2

HEAD_DIM = 64
ATTN_W = D_MODEL // 2
N_Q_HEADS = ATTN_W // HEAD_DIM
N_KV_HEADS = N_Q_HEADS // 4
GQA_GROUP = N_Q_HEADS // N_KV_HEADS
KV_W = N_KV_HEADS * HEAD_DIM
CONV_W = D_MODEL // 4
CONV_HEADS = CONV_W // HEAD_DIM
CONV_K = 3
FFT_W = D_MODEL // 4
FFT_GROUP_DIM = 64
FFT_GROUPS = FFT_W // FFT_GROUP_DIM
MIX_W = ATTN_W + CONV_W + FFT_W
IN_SIZES = (ATTN_W, KV_W, KV_W, ATTN_W, CONV_W, CONV_W, CONV_W, CONV_W, FFT_W, FFT_W)
IN_W = sum(IN_SIZES)
GRID_W = 64
ROPE_THETA = 10000.0
ROPE_HALF = HEAD_DIM // 2
Q_BLOCK = 128
RMS_EPS = 1e-6
LN_EPS = 1e-5
DEEPNORM_ALPHA = (2 * DEPTH) ** 0.25
DEEPNORM_BETA = (8 * DEPTH) ** -0.25
ADA_SCALE = 0.1


def _layer_norm(x, eps):
    xf = x.astype(jnp.float32)
    mu = jnp.mean(xf, axis=-1, keepdims=True)
    xc = xf - mu
    var = jnp.mean(xc * xc, axis=-1, keepdims=True)
    return (xc * lax.rsqrt(var + eps)).astype(x.dtype)

def _rms_norm(x, gain):
    xf = x.astype(jnp.float32)
    y = xf * lax.rsqrt(jnp.mean(xf * xf, axis=-1, keepdims=True) + RMS_EPS)
    return (y * gain.astype(jnp.float32)).astype(x.dtype)

def _axial_angles(seq_len):
    rows = seq_len // GRID_W
    row_pos = jnp.repeat(jnp.arange(rows, dtype=jnp.float32), GRID_W)
    col_pos = jnp.tile(jnp.arange(GRID_W, dtype=jnp.float32), rows)
    inv_freq = 1.0 / (ROPE_THETA ** (jnp.arange(0, ROPE_HALF, 2, dtype=jnp.float32) / ROPE_HALF))
    return row_pos[:, None] * inv_freq, col_pos[:, None] * inv_freq

def _rope_half(x, ang):
    cos = jnp.cos(ang)[:, None, :].astype(x.dtype)
    sin = jnp.sin(ang)[:, None, :].astype(x.dtype)
    x1, x2 = jnp.split(x, 2, axis=-1)
    return jnp.concatenate([x1 * cos - x2 * sin, x2 * cos + x1 * sin], axis=-1)

def _axial_rope(x, row_ang, col_ang):
    xr, xc = jnp.split(x, 2, axis=-1)
    return jnp.concatenate([_rope_half(xr, row_ang), _rope_half(xc, col_ang)], axis=-1)

def _attention(q, k, v):
    b, s = q.shape[0], q.shape[1]
    nb = s // Q_BLOCK
    scale = HEAD_DIM ** -0.5
    qg = q.reshape(b, nb, Q_BLOCK, N_KV_HEADS, GQA_GROUP, HEAD_DIM).transpose(1, 0, 2, 3, 4, 5)

    def block(qb):
        scores = jnp.einsum('bqkgd,bskd->bkgqs', qb, k,
                            preferred_element_type=jnp.float32) * scale
        p = jax.nn.softmax(scores, axis=-1).astype(v.dtype)
        return jnp.einsum('bkgqs,bskd->bqkgd', p, v)

    o = lax.map(block, qg)
    return o.transpose(1, 0, 2, 3, 4, 5).reshape(b, s, ATTN_W)

def _short_conv(u, w):
    s = u.shape[1]
    pad = CONV_K // 2
    up = jnp.pad(u, ((0, 0), (pad, pad), (0, 0)))
    return sum(up[:, j:j + s, :] * w[j] for j in range(CONV_K))

def _fourier(u, f_mix):
    b, s = u.shape[0], u.shape[1]
    ug = u.reshape(b, s, FFT_GROUPS, FFT_GROUP_DIM).astype(jnp.float32)
    f = jnp.fft.fft2(ug, axes=(1, 3), norm='ortho').real.astype(u.dtype)
    f = jnp.einsum('bsgc,gcd->bsgd', f, f_mix)
    return f.reshape(b, s, FFT_W)

def _split_indices():
    return np.cumsum(np.array(IN_SIZES))[:-1].tolist()

def first_inputs(seed: int = 0) -> dict:
    key = jax.random.key(seed)
    ks = jax.random.split(key, 12)
    f32 = jnp.float32
    x = jax.random.normal(ks[0], (BATCH, SEQ, D_MODEL), f32)
    c = jax.random.normal(ks[1], (BATCH, D_MODEL), f32)
    w_ada = jax.random.normal(ks[2], (DEPTH, D_MODEL, 3 * D_MODEL), f32) * (D_MODEL ** -0.5) * ADA_SCALE
    b_ada = jax.random.normal(ks[3], (DEPTH, 3 * D_MODEL), f32) * 0.01
    w_in = jax.random.normal(ks[4], (DEPTH, D_MODEL, IN_W), f32) * (D_MODEL ** -0.5)
    q_gain = 1.0 + 0.05 * jax.random.normal(ks[5], (DEPTH, HEAD_DIM), f32)
    k_gain = 1.0 + 0.05 * jax.random.normal(ks[6], (DEPTH, HEAD_DIM), f32)
    conv_w = jax.random.normal(ks[7], (DEPTH, CONV_K, CONV_W), f32) * (CONV_K ** -0.5)
    f_mix = jax.random.normal(ks[8], (DEPTH, FFT_GROUPS, FFT_GROUP_DIM, FFT_GROUP_DIM), f32) * (FFT_GROUP_DIM ** -0.5)
    w_out = jax.random.normal(ks[9], (DEPTH, MIX_W, D_MODEL), f32) * (MIX_W ** -0.5) * DEEPNORM_BETA
    ln_g = 1.0 + 0.05 * jax.random.normal(ks[10], (DEPTH, D_MODEL), f32)
    ln_b = 0.01 * jax.random.normal(ks[11], (DEPTH, D_MODEL), f32)
    return {"x": x, "c": c, "w_ada": w_ada, "b_ada": b_ada, "w_in": w_in,
            "q_gain": q_gain, "k_gain": k_gain, "conv_w": conv_w, "f_mix": f_mix,
            "w_out": w_out, "ln_g": ln_g, "ln_b": ln_b}

def first_block(x, c, w_ada, b_ada, w_in, q_gain, k_gain, conv_w, f_mix, w_out, ln_g, ln_b):
    b, s, _ = x.shape
    row_ang, col_ang = _axial_angles(s)
    split_idx = _split_indices()
    for l in range(DEPTH):
        mod = c @ w_ada[l] + b_ada[l]
        shift, scale, gate = jnp.split(mod, 3, axis=-1)
        h = _layer_norm(x, LN_EPS) * (1.0 + scale[:, None, :]) + shift[:, None, :]

        proj = h @ w_in[l]
        q, k, v, g_a, cu, cb, cc, g_c, fu, g_f = jnp.split(proj, split_idx, axis=-1)

        q = _axial_rope(_rms_norm(q.reshape(b, s, N_Q_HEADS, HEAD_DIM), q_gain[l]), row_ang, col_ang)
        k = _axial_rope(_rms_norm(k.reshape(b, s, N_KV_HEADS, HEAD_DIM), k_gain[l]), row_ang, col_ang)
        v = v.reshape(b, s, N_KV_HEADS, HEAD_DIM)
        y_attn = _attention(q, k, v) * jax.nn.silu(g_a)

        y_conv = cb * _short_conv(cc * cu, conv_w[l]) * jax.nn.silu(g_c)

        y_four = _fourier(fu, f_mix[l]) * jax.nn.silu(g_f)

        y = jnp.concatenate([y_attn, y_conv, y_four], axis=-1) @ w_out[l]

        x = _layer_norm(DEEPNORM_ALPHA * x + (1.0 + gate[:, None, :]) * y, LN_EPS) * ln_g[l] + ln_b[l]
    return x


N_EVEN = (DEPTH + 1) // 2
N_ODD = DEPTH // 2
D_FF = 2816
FFN_RES = 0.5
NORM_EPS = 1e-6
CHUNK = 64
CONV_W_2 = 4

GLA_HEADS = 4
GLA_DK = 64
GLA_DV = 128
GLA_LORA = 16
GLA_GATE_NORM = 16.0
GLA_QK = GLA_HEADS * GLA_DK
GLA_V = GLA_HEADS * GLA_DV
GDN_HEADS = 4
GDN_DK = 128
GDN_DV = 128
GDN_QK = GDN_HEADS * GDN_DK
GDN_V = GDN_HEADS * GDN_DV
GDN_CONV_CH = 2 * GDN_QK + GDN_V
RWKV_HEADS = 8
RWKV_N = 64
RWKV_W = RWKV_HEADS * RWKV_N
RWKV_W_LORA = 64
RWKV_A_LORA = 64
RWKV_G_LORA = 128
RWKV_GN_EPS = 64e-5
RWKV_SHIFT = 3 * RWKV_W + RWKV_W_LORA + RWKV_A_LORA + RWKV_G_LORA
LRU_WIDTH = 512
LRU_BLOCKS = 8
LRU_BW = LRU_WIDTH // LRU_BLOCKS
LRU_C = 8.0

EVEN_SPLITS = (GLA_QK, GLA_QK, GLA_V, GLA_V, GLA_LORA, GDN_CONV_CH, GDN_V, GDN_HEADS, GDN_HEADS)
EVEN_IN = 2 * GLA_QK + 2 * GLA_V + GLA_LORA + GDN_CONV_CH + GDN_V + 2 * GDN_HEADS
EVEN_OUT = GLA_V + GDN_V
RWKV_SPLITS = (RWKV_W, RWKV_W, RWKV_W, RWKV_W_LORA, RWKV_A_LORA, RWKV_G_LORA)
ODD_IN = RWKV_SHIFT + 2 * LRU_WIDTH
ODD_OUT = RWKV_W + LRU_WIDTH


def _split(x, sizes):
    out, o = [], 0
    for s in sizes:
        out.append(x[..., o:o + s])
        o += s
    return out

def _rmsnorm(x, w):
    xf = x.astype(jnp.float32)
    y = xf * lax.rsqrt(jnp.mean(xf * xf, -1, keepdims=True) + NORM_EPS) * w
    return y.astype(x.dtype)

def _heads(x, n_heads):
    return x.reshape(x.shape[:-1] + (n_heads, x.shape[-1] // n_heads))

def _l2norm(x):
    xf = x.astype(jnp.float32)
    return xf * lax.rsqrt(jnp.sum(xf * xf, -1, keepdims=True) + NORM_EPS)

def _head_rmsnorm(x, n_heads, w):
    xh = _heads(x.astype(jnp.float32), n_heads)
    xh = xh * lax.rsqrt(jnp.mean(xh * xh, -1, keepdims=True) + NORM_EPS) * w
    return xh.reshape(x.shape).astype(x.dtype)

def _swiglu(x, w_gate, w_up, w_down):
    return (jax.nn.silu(x @ w_gate) * (x @ w_up)) @ w_down

def _causal_dwconv(x, w):
    K, T = w.shape[0], x.shape[1]
    xp = jnp.pad(x, ((0, 0), (K - 1, 0), (0, 0)))
    y = xp[:, 0:T] * w[0]
    for j in range(1, K):
        y = y + xp[:, j:j + T] * w[j]
    return y

def _token_shift(x):
    return jnp.pad(x, ((0, 0), (1, 0), (0, 0)))[:, :-1]

def _to_chunks(x):
    B, T, H, d = x.shape
    return x.reshape(B, T // CHUNK, CHUNK, H, d).transpose(0, 3, 1, 2, 4)

def _from_chunks(o):
    B, H, N, C, d = o.shape
    return o.transpose(0, 2, 3, 1, 4).reshape(B, N * C, H * d)

def _gla_chunked(q, k, v, log_a):
    C = q.shape[-2]
    causal = jnp.tril(jnp.ones((C, C), bool))
    b = jnp.cumsum(log_a, axis=-2)
    q_e = q * jnp.exp(b)
    att = jnp.where(causal, jnp.einsum('bhncd,bhnsd->bhncs', q_e, k * jnp.exp(-b)), 0.0)
    o_intra = jnp.einsum('bhncs,bhnsv->bhncv', att, v)
    b_last = b[..., -1:, :]
    k_dec = k * jnp.exp(b_last - b)
    a_last = jnp.exp(b_last[..., 0, :])

    def step(S, xs):
        qe, kd, vv, al = xs
        o = jnp.einsum('bhcd,bhdv->bhcv', qe, S)
        S = S * al[..., None] + jnp.einsum('bhcd,bhcv->bhdv', kd, vv)
        return S, o

    B, H, _, _, dk = q.shape
    S0 = jnp.zeros((B, H, dk, v.shape[-1]), q.dtype)
    _, o_inter = lax.scan(step, S0, tuple(jnp.moveaxis(t, 2, 0) for t in (q_e, k_dec, v, a_last)))
    return o_intra + jnp.moveaxis(o_inter, 0, 2)

def _gated_delta_chunked(q, k, v, g, beta):
    C, dv = q.shape[-2], v.shape[-1]
    tril = jnp.tril(jnp.ones((C, C), bool))
    strict = jnp.tril(jnp.ones((C, C), bool), -1)
    gc = jnp.cumsum(g, axis=-1)
    diff = gc[..., :, None] - gc[..., None, :]
    decay = jnp.where(tril, jnp.exp(jnp.where(tril, diff, 0.0)), 0.0)
    kb = k * beta[..., None]
    L = jnp.where(strict, jnp.einsum('bhncd,bhnsd->bhncs', kb, k) * decay, 0.0)
    rhs = jnp.concatenate([v * beta[..., None], kb * jnp.exp(gc)[..., None]], -1)
    sol = lax.linalg.triangular_solve(L + jnp.eye(C, dtype=L.dtype), rhs,
                                      left_side=True, lower=True, unit_diagonal=True)
    u, w = sol[..., :dv], sol[..., dv:]
    att = jnp.where(tril, jnp.einsum('bhncd,bhnsd->bhncs', q, k) * decay, 0.0)
    q_e = q * jnp.exp(gc)[..., None]
    k_dec = k * jnp.exp(gc[..., -1:] - gc)[..., None]
    g_last = jnp.exp(gc[..., -1])

    def step(S, xs):
        qe, kd, uu, ww, aa, gl = xs
        v_new = uu - jnp.einsum('bhcd,bhdv->bhcv', ww, S)
        o = jnp.einsum('bhcd,bhdv->bhcv', qe, S) + jnp.einsum('bhcs,bhsv->bhcv', aa, v_new)
        S = S * gl[..., None, None] + jnp.einsum('bhcd,bhcv->bhdv', kd, v_new)
        return S, o

    B, H, _, _, dk = q.shape
    S0 = jnp.zeros((B, H, dk, dv), q.dtype)
    _, o = lax.scan(step, S0, tuple(jnp.moveaxis(t, 2, 0) for t in (q_e, k_dec, u, w, att, g_last)))
    return jnp.moveaxis(o, 0, 2)

def _rwkv7_scan(r, w, k, v, kk, a):
    B, T, H, N = r.shape

    def step(S, xs):
        rt, wt, kt, vt, kkt, at = xs
        sa = jnp.einsum('bhij,bhj->bhi', S, -kkt)
        S = S * wt[:, :, None, :] + sa[..., None] * (kkt * at)[:, :, None, :] + vt[..., None] * kt[:, :, None, :]
        return S, jnp.einsum('bhij,bhj->bhi', S, rt)

    S0 = jnp.zeros((B, H, N, N), r.dtype)
    _, y = lax.scan(step, S0, tuple(jnp.moveaxis(t, 1, 0) for t in (r, w, k, v, kk, a)))
    return jnp.moveaxis(y, 0, 1)

def _linear_scan(a, b):
    def combine(c1, c2):
        a1, b1 = c1
        a2, b2 = c2
        return a1 * a2, a2 * b1 + b2
    _, h = lax.associative_scan(combine, (a, b), axis=1)
    return h

def _even_mixer(h, w_in, w_out, gla_lora_w2, gla_lora_b, gla_norm, gdn_conv, gdn_a_log, gdn_dt_bias, gdn_norm):
    f32 = jnp.float32
    p = h @ w_in
    gq, gk, gv, gg, glr, dqkv, dz, da, db = _split(p, EVEN_SPLITS)
    log_a = jax.nn.log_sigmoid((glr @ gla_lora_w2 + gla_lora_b).astype(f32)) / GLA_GATE_NORM
    o_gla = _gla_chunked(_to_chunks(_heads(gq.astype(f32) * GLA_DK ** -0.5, GLA_HEADS)),
                         _to_chunks(_heads(gk.astype(f32), GLA_HEADS)),
                         _to_chunks(_heads(gv.astype(f32), GLA_HEADS)),
                         _to_chunks(_heads(log_a, GLA_HEADS)))
    y_gla = _head_rmsnorm(_from_chunks(o_gla).astype(h.dtype), GLA_HEADS, gla_norm) * jax.nn.silu(gg)
    c = jax.nn.silu(_causal_dwconv(dqkv, gdn_conv))
    cq, ck, cv = _split(c, (GDN_QK, GDN_QK, GDN_V))
    q = _l2norm(_heads(cq, GDN_HEADS)) * GDN_DK ** -0.5
    k = _l2norm(_heads(ck, GDN_HEADS))
    v = _heads(cv.astype(f32), GDN_HEADS)
    beta = jax.nn.sigmoid(db.astype(f32))
    g = -jnp.exp(gdn_a_log.astype(f32)) * jax.nn.softplus((da + gdn_dt_bias).astype(f32))
    o_gdn = _gated_delta_chunked(_to_chunks(q), _to_chunks(k), _to_chunks(v),
                                 _to_chunks(g[..., None])[..., 0], _to_chunks(beta[..., None])[..., 0])
    y_gdn = _head_rmsnorm(_from_chunks(o_gdn).astype(h.dtype), GDN_HEADS, gdn_norm) * jax.nn.silu(dz)
    return jnp.concatenate([y_gla, y_gdn], -1) @ w_out

def _odd_mixer(h, w_in, w_out, rwkv_mu, rwkv_w0, rwkv_w2, rwkv_a0, rwkv_a2, rwkv_g2, rwkv_k_k, rwkv_k_a,
               rwkv_r_k, rwkv_ln_w, rwkv_ln_b, lru_conv_w, lru_conv_b, lru_wa, lru_ba, lru_wx, lru_bx, lru_lambda):
    f32 = jnp.float32
    B, T, _ = h.shape
    p = h @ w_in
    ps, lx, ly = _split(p, (RWKV_SHIFT, LRU_WIDTH, LRU_WIDTH))
    ps = ps + (_token_shift(ps) - ps) * rwkv_mu
    r, k, v, wl, al, gl = _split(ps, RWKV_SPLITS)
    w = -jax.nn.softplus(-(rwkv_w0 + jnp.tanh(wl) @ rwkv_w2).astype(f32)) - 0.5
    decay = jnp.exp(-jnp.exp(w))
    a = jax.nn.sigmoid(rwkv_a0 + al @ rwkv_a2)
    g = jax.nn.sigmoid(gl) @ rwkv_g2
    kk = _l2norm(_heads(k * rwkv_k_k, RWKV_HEADS))
    k = k * (1.0 + (a - 1.0) * rwkv_k_a)
    rh, kh, vh = _heads(r, RWKV_HEADS), _heads(k, RWKV_HEADS), _heads(v, RWKV_HEADS)
    y = _rwkv7_scan(rh.astype(f32), _heads(decay, RWKV_HEADS), kh.astype(f32), vh.astype(f32),
                    kk, _heads(a, RWKV_HEADS).astype(f32))
    mu = jnp.mean(y, -1, keepdims=True)
    var = jnp.mean(jnp.square(y - mu), -1, keepdims=True)
    y = ((y - mu) * lax.rsqrt(var + RWKV_GN_EPS)).reshape(B, T, RWKV_W) * rwkv_ln_w + rwkv_ln_b
    bonus = (jnp.sum(rh * kh * rwkv_r_k, -1, keepdims=True) * vh).reshape(B, T, RWKV_W)
    y_rwkv = ((y.astype(h.dtype) + bonus) * g)
    xb = _causal_dwconv(lx, lru_conv_w) + lru_conv_b
    xblk = _heads(xb, LRU_BLOCKS)
    gate_r = jax.nn.sigmoid(jnp.einsum('btki,kij->btkj', xblk, lru_wa).reshape(B, T, LRU_WIDTH) + lru_ba).astype(f32)
    gate_i = jax.nn.sigmoid(jnp.einsum('btki,kij->btkj', xblk, lru_wx).reshape(B, T, LRU_WIDTH) + lru_bx).astype(f32)
    log_a = -LRU_C * gate_r * jax.nn.softplus(-lru_lambda.astype(f32))
    mult = jnp.sqrt(jnp.maximum(-jnp.expm1(2.0 * log_a), 0.0))
    hl = _linear_scan(jnp.exp(log_a), mult * gate_i * xb.astype(f32))
    y_lru = hl.astype(h.dtype) * jax.nn.gelu(ly)
    return jnp.concatenate([y_rwkv, y_lru], -1) @ w_out

def second_inputs(seed: int = 0) -> dict:
    key = jax.random.key(seed)
    ks = jax.random.split(key, 34)
    f32 = jnp.float32

    def nrm(i, shape, scale):
        return jax.random.normal(ks[i], shape, f32) * scale

    def uni(i, shape, lo, hi):
        return jax.random.uniform(ks[i], shape, f32, lo, hi)

    E, O = N_EVEN, N_ODD
    dt = jnp.exp(uni(12, (E, GDN_HEADS), math.log(1e-3), math.log(1e-1)))
    s = uni(33, (O, LRU_WIDTH), 0.9, 0.999) ** (1.0 / LRU_C)
    return {
        'x': nrm(0, (BATCH, SEQ, D_MODEL), 1.0),
        'norm_w': 1.0 + nrm(1, (DEPTH, 6, D_MODEL), 0.05),
        'ffn_w_gate': nrm(2, (DEPTH, 2, D_MODEL, D_FF), D_MODEL ** -0.5),
        'ffn_w_up': nrm(3, (DEPTH, 2, D_MODEL, D_FF), D_MODEL ** -0.5),
        'ffn_w_down': nrm(4, (DEPTH, 2, D_FF, D_MODEL), D_FF ** -0.5),
        'even_w_in': nrm(5, (E, D_MODEL, EVEN_IN), D_MODEL ** -0.5),
        'even_w_out': nrm(6, (E, EVEN_OUT, D_MODEL), EVEN_OUT ** -0.5),
        'gla_lora_w2': nrm(7, (E, GLA_LORA, GLA_QK), GLA_LORA ** -0.5),
        'gla_lora_b': nrm(8, (E, GLA_QK), 0.1),
        'gla_norm': 1.0 + nrm(9, (E, GLA_DV), 0.05),
        'gdn_conv': nrm(10, (E, CONV_W_2, GDN_CONV_CH), CONV_W_2 ** -0.5),
        'gdn_a_log': jnp.log(uni(11, (E, GDN_HEADS), 1.0, 16.0)),
        'gdn_dt_bias': dt + jnp.log(-jnp.expm1(-dt)),
        'gdn_norm': 1.0 + nrm(13, (E, GDN_DV), 0.05),
        'odd_w_in': nrm(14, (O, D_MODEL, ODD_IN), D_MODEL ** -0.5),
        'odd_w_out': nrm(15, (O, ODD_OUT, D_MODEL), ODD_OUT ** -0.5),
        'rwkv_mu': uni(16, (O, RWKV_SHIFT), 0.0, 1.0),
        'rwkv_w0': -6.5 + 5.0 * jnp.linspace(0.0, 1.0, RWKV_W, dtype=f32) ** 0.85 + nrm(17, (O, RWKV_W), 0.05),
        'rwkv_w2': nrm(18, (O, RWKV_W_LORA, RWKV_W), RWKV_W_LORA ** -0.5),
        'rwkv_a0': nrm(19, (O, RWKV_W), 0.1),
        'rwkv_a2': nrm(20, (O, RWKV_A_LORA, RWKV_W), RWKV_A_LORA ** -0.5),
        'rwkv_g2': nrm(21, (O, RWKV_G_LORA, RWKV_W), RWKV_G_LORA ** -0.5),
        'rwkv_k_k': 0.85 + nrm(22, (O, RWKV_W), 0.05),
        'rwkv_k_a': 1.0 + nrm(23, (O, RWKV_W), 0.05),
        'rwkv_r_k': nrm(24, (O, RWKV_HEADS, RWKV_N), 0.1),
        'rwkv_ln_w': 1.0 + nrm(25, (O, RWKV_W), 0.05),
        'rwkv_ln_b': nrm(26, (O, RWKV_W), 0.02),
        'lru_conv_w': nrm(27, (O, CONV_W_2, LRU_WIDTH), CONV_W_2 ** -0.5),
        'lru_conv_b': nrm(28, (O, LRU_WIDTH), 0.02),
        'lru_wa': nrm(29, (O, LRU_BLOCKS, LRU_BW, LRU_BW), LRU_BW ** -0.5),
        'lru_ba': nrm(30, (O, LRU_WIDTH), 0.02),
        'lru_wx': nrm(31, (O, LRU_BLOCKS, LRU_BW, LRU_BW), LRU_BW ** -0.5),
        'lru_bx': nrm(32, (O, LRU_WIDTH), 0.02),
        'lru_lambda': jnp.log(s) - jnp.log1p(-s),
    }

def second_block(x, norm_w, ffn_w_gate, ffn_w_up, ffn_w_down, even_w_in, even_w_out, gla_lora_w2, gla_lora_b,
              gla_norm, gdn_conv, gdn_a_log, gdn_dt_bias, gdn_norm, odd_w_in, odd_w_out, rwkv_mu, rwkv_w0,
              rwkv_w2, rwkv_a0, rwkv_a2, rwkv_g2, rwkv_k_k, rwkv_k_a, rwkv_r_k, rwkv_ln_w, rwkv_ln_b,
              lru_conv_w, lru_conv_b, lru_wa, lru_ba, lru_wx, lru_bx, lru_lambda):
    for i in range(DEPTH):
        j = i // 2
        hh = _rmsnorm(x, norm_w[i, 0])
        x = x + FFN_RES * _rmsnorm(_swiglu(hh, ffn_w_gate[i, 0], ffn_w_up[i, 0], ffn_w_down[i, 0]), norm_w[i, 1])
        hh = _rmsnorm(x, norm_w[i, 2])
        if i % 2 == 0:
            m = _even_mixer(hh, even_w_in[j], even_w_out[j], gla_lora_w2[j], gla_lora_b[j], gla_norm[j],
                            gdn_conv[j], gdn_a_log[j], gdn_dt_bias[j], gdn_norm[j])
        else:
            m = _odd_mixer(hh, odd_w_in[j], odd_w_out[j], rwkv_mu[j], rwkv_w0[j], rwkv_w2[j], rwkv_a0[j],
                           rwkv_a2[j], rwkv_g2[j], rwkv_k_k[j], rwkv_k_a[j], rwkv_r_k[j], rwkv_ln_w[j],
                           rwkv_ln_b[j], lru_conv_w[j], lru_conv_b[j], lru_wa[j], lru_ba[j], lru_wx[j],
                           lru_bx[j], lru_lambda[j])
        x = x + _rmsnorm(m, norm_w[i, 3])
        hh = _rmsnorm(x, norm_w[i, 4])
        x = x + FFN_RES * _rmsnorm(_swiglu(hh, ffn_w_gate[i, 1], ffn_w_up[i, 1], ffn_w_down[i, 1]), norm_w[i, 5])
    return x


def setup_inputs(seed=0):
    out = dict(first_inputs(seed))
    for name, value in second_inputs(seed + 1).items():
        if name != "x":
            out[name + "_2"] = value
    return out


def reference(
    x, c, w_ada, b_ada, w_in, q_gain, k_gain, conv_w, f_mix, w_out, ln_g, ln_b, norm_w_2,
    ffn_w_gate_2, ffn_w_up_2, ffn_w_down_2, even_w_in_2, even_w_out_2, gla_lora_w2_2,
    gla_lora_b_2, gla_norm_2, gdn_conv_2, gdn_a_log_2, gdn_dt_bias_2, gdn_norm_2, odd_w_in_2,
    odd_w_out_2, rwkv_mu_2, rwkv_w0_2, rwkv_w2_2, rwkv_a0_2, rwkv_a2_2, rwkv_g2_2, rwkv_k_k_2,
    rwkv_k_a_2, rwkv_r_k_2, rwkv_ln_w_2, rwkv_ln_b_2, lru_conv_w_2, lru_conv_b_2, lru_wa_2,
    lru_ba_2, lru_wx_2, lru_bx_2, lru_lambda_2,
):
    x = first_block(
        x, c, w_ada, b_ada, w_in, q_gain, k_gain, conv_w, f_mix, w_out, ln_g, ln_b,
    )
    return second_block(
        x, norm_w_2, ffn_w_gate_2, ffn_w_up_2, ffn_w_down_2, even_w_in_2, even_w_out_2,
        gla_lora_w2_2, gla_lora_b_2, gla_norm_2, gdn_conv_2, gdn_a_log_2, gdn_dt_bias_2,
        gdn_norm_2, odd_w_in_2, odd_w_out_2, rwkv_mu_2, rwkv_w0_2, rwkv_w2_2, rwkv_a0_2,
        rwkv_a2_2, rwkv_g2_2, rwkv_k_k_2, rwkv_k_a_2, rwkv_r_k_2, rwkv_ln_w_2, rwkv_ln_b_2,
        lru_conv_w_2, lru_conv_b_2, lru_wa_2, lru_ba_2, lru_wx_2, lru_bx_2, lru_lambda_2,
    )


_drawn_inputs = setup_inputs


def setup_inputs(seed=0):
    import zlib

    import numpy as np

    out = dict(_drawn_inputs(seed))
    spreads = {}
    factors = {'b_ada': 4.133,
     'q_gain': 8.0,
     'k_gain': 8.0,
     'rwkv_a0_2': 3.509,
     'rwkv_k_k_2': 12.143,
     'rwkv_ln_w_2': 2.96,
     'rwkv_ln_b_2': 6.693,
     'lru_ba_2': 64.0,
     'lru_bx_2': 45.066,
     'lru_conv_b_2': 3.206}
    for name, (base, spread) in spreads.items():
        noise = np.random.default_rng([zlib.crc32(name.encode()), seed]).standard_normal(out[name].shape)
        drawn = base * np.exp(spread * noise) if base else spread * noise
        out[name] = __import__('jax').numpy.asarray(drawn.astype(out[name].dtype))
    for name, factor in factors.items():
        out[name] = (out[name] * factor).astype(out[name].dtype)
    return out
```

```python
from contextlib import ExitStack

import numpy as np

import concourse.bass as bass
from concourse import mybir

F32 = mybir.dt.float32
ALU = mybir.AluOpType
ACT = mybir.ActivationFunctionType
AX_X = mybir.AxisListType.X

P = 128
D = 1024
T = 512
KT = D // P
TT = T // P
DEPTH = 2
ALPHA = (2 * DEPTH) ** 0.25
CH = 64
NCH = T // CH
D_FF = 2816
FT = D_FF // P
KD = FT // 2
SLOTS = 4
UNIT = KT * P
UNIT_D = KD * P
LEVELS = 6
DECAY = float(np.exp(-0.5))

Q0, K0, V0, GA0, CU0, CB0, CC0, GC0, FU0, GF0, N_FIRST = 0, 4, 5, 6, 10, 12, 14, 16, 18, 20, 22
GQ0, GK0, GV0, GG0, SM0, DQ0, DK0, DV0, DZ0, N_EVEN = 0, 2, 4, 8, 12, 13, 17, 21, 25, 29
GLR_ROW, DA_ROW, DB_ROW, EG_ROW, ED_ROW = 0, 32, 64, 0, 96
R0, RK0, RV0, WA0, GL0, LX0, LY0, N_ODD = 0, 4, 8, 12, 13, 14, 18, 22

STREAM = [("ada0", 24, "k"), ("ada1", 24, "k")]
for _l in range(DEPTH):
    STREAM += [(f"first{_l}", N_FIRST, "k"), (f"firstout{_l}", KT, "k")]
for _i in range(DEPTH):
    STREAM += [(f"ffn{_i}0", 2 * FT, "k"), (f"down{_i}0", 2 * KT, "d"),
               (f"mix{_i}", (N_EVEN, N_ODD)[_i % 2], "k"), (f"mixout{_i}", KT, "k"),
               (f"ffn{_i}1", 2 * FT, "k"), (f"down{_i}1", 2 * KT, "d")]
UNIT0, _n = {}, 0
for _name, _count, _kind in STREAM:
    UNIT0[_name] = _n
    _n += _count
IN_ARRAY, _m = {}, {"k": 0, "d": 0}
for _name, _count, _kind in STREAM:
    IN_ARRAY[_name] = _m[_kind]
    _m[_kind] += _count
N_K, N_D = _m["k"], _m["d"]

VECS = [("c", 8), ("bada", 48), ("qg", 2), ("kg", 2), ("cw", 12), ("lng", 16), ("lnb", 16),
        ("nw", 96), ("lorab", 2), ("glan", 1), ("gdnconv", 48), ("alog", 1), ("dtb", 1), ("gdnn", 1),
        ("mu", 14), ("w0", 4), ("a0", 4), ("kk", 4), ("ka", 4), ("rk", 4), ("lnw", 4), ("lnbb", 4),
        ("lconv", 16), ("lconvb", 4), ("lba", 4), ("lbx", 4), ("lam", 4),
        ("eps6", 1), ("eps5", 1), ("epsg", 1), ("one", 1)]
VCOL, _n = {}, 0
for _name, _count in VECS:
    VCOL[_name] = _n
    _n += _count
NV = _n

CSTS = [("cos", T), ("sin", T), ("reset", T), ("ident", P), ("incl", P), ("strict", P),
        *[(f"lev{b}", P) for b in range(LEVELS)], ("onesD", P), ("ones128", P), ("ones1", P),
        ("blk1", P), ("blk64", P), ("perm", P), ("sel", 4 * P), ("c64", P), ("s64", P)]
CCOL, _n = {}, 0
for _name, _count in CSTS:
    CCOL[_name] = (_n, _count)
    _n += _count
NC = _n

SMALLS = [("fmix", 2 * 2 * P), ("lora", 2 * P), ("wa2", 4 * P), ("g2", 4 * P), ("lwa", 4 * P), ("lwx", 4 * P)]
SCOL, _n = {}, 0
for _name, _count in SMALLS:
    SCOL[_name] = _n
    _n += _count
NS = _n


def step_counter(name, sem, known, seen):
    count, inside = [0], []

    def signal(step=None):
        count[0] += 1
        if step is not None:
            assert (name, step) not in seen, step
            seen[name, step] = (count[0], 0, 1)
            inside.append(step)
        return sem, 1

    def so_far():
        return sem, count[0]

    def begin_loop():
        inside[:] = []
        return count[0]

    def end_loop(first, rounds):
        body = count[0] - first
        for step in inside:
            seen[name, step] = (seen[name, step][0], body, rounds)
        count[0] = first + body * rounds

    def done(*step, i=None, lag=0):
        first, body, rounds = known.get((name, step if len(step) > 1 else step[0]), (1000, 0, 1))
        if i is None:
            return sem, first + body * (rounds - 1)
        assert not known or first - lag * body > 0, step
        return sem, i * body + (first - lag * body)

    return signal, so_far, begin_loop, end_loop, done


def write_program(nc, known, x_in, w_k, w_d, vec_in, cst_in, small_in, dft_in, out):
    with ExitStack() as ctx:
        def sb(name, shape):
            return ctx.enter_context(nc.sbuf_tensor(name, shape, F32))

        def sem(name):
            return ctx.enter_context(nc.semaphore(name))

        X = sb("residual", [P, KT, T])
        H = sb("normed", [P, KT, T])
        BIG = sb("work", [P, 44, T])
        RING = sb("ring", [P, SLOTS, UNIT_D])
        CST = sb("constants", [P, NC])
        VEC = sb("vectors", [P, NV])
        SMALL = sb("small_weights", [P, NS])
        GATE = sb("silu_gate", [P, 2, T])
        RSTD = sb("rstd", [P, 2, T])
        MOD = sb("modulation", [P, 2, 24])
        STAT = sb("softmax_stats", [P, 4, 32])
        LRUV = sb("lru_vectors", [P, 16])
        STATE = sb("state", [P, 4 * P])
        PS = [ctx.enter_context(nc.psum_tensor(f"bank{i}", [P, T], F32)) for i in range(8)]

        w_loaded = [sem(f"w_loaded{i}") for i in range(SLOTS)]
        unit_used = sem("unit_used")
        tile_copied = sem("tile_copied")
        consts_in = sem("consts_in")
        dft_in_s = sem("dft_in")
        out_stored = sem("out_stored")
        seen = {}
        pe_signal, pe_so_far, pe_begin_loop, pe_end_loop, pe_done = step_counter("pe", sem("pe_steps"), known, seen)
        act_signal, act_so_far, act_begin_loop, act_end_loop, act_done = step_counter("act", sem("act_steps"), known, seen)
        dve_signal, dve_so_far, dve_begin_loop, dve_end_loop, dve_done = step_counter("dve", sem("dve_steps"), known, seen)

        def v(name, j=0):
            return VEC[:, VCOL[name] + j:VCOL[name] + j + 1]

        def cst(name, a=0, b=None):
            c, n = CCOL[name]
            return CST[:, c + a:c + (n if b is None else b)]

        def tile(i):
            return BIG[:, i, :]

        def by_tt(ap):
            return ap.rearrange("p (t c) -> p t c", t=TT)

        def by_chunk(ap):
            return ap.rearrange("p (n c) -> p n c", c=CH)

        def mask4(name):
            return cst(name).unsqueeze(1).broadcast_to([P, TT, P])

        def col(tt, w=P):
            return slice(tt * w, tt * w + w)

        def loaded(u, i=None, per=1):
            value = 16 * (u // SLOTS + 1)
            return w_loaded[u % SLOTS], value if i is None else i * (16 * per) + value

        COPIED, n_copied = {}, 0
        for name, count, _ in STREAM:
            if name.startswith(("first", "mix")):
                COPIED[name] = n_copied
                n_copied += count

        def token_major(name):
            if name in ("first0", "first1"):
                return V0, V0 + 1
            if name == "mix0":
                return GV0, GV0 + 4
            return 0, 0

        def segments(name):
            count = dict((n, c) for n, c, _ in STREAM)[name]
            first, end_tm = token_major(name)
            runs, at = [], 0
            for end, is_tm in ((first, False), (end_tm, True), (count, False)):
                if (end - at) // SLOTS > 1:
                    g = (end - at) // SLOTS
                    runs.append((at, g, SLOTS, is_tm))
                    at += g * SLOTS
                if end > at:
                    runs.append((at, 1, end - at, is_tm))
                    at = end
            return runs

        def v4(name):
            return VEC[:, VCOL[name]:VCOL[name] + 4]

        GATT = [29, 30, 33, 34]
        HSQ = {"gla": [35, 36, 41, 42], "gdn": [0, 1, 2, 3]}

        def gla_state(j, c):
            return tile(37 + 2 * j + (c - 1) // 4)[:, col((c - 1) % 4)]

        INV = {"gdn": ([tile(i) for i in (17, 18, 19, 20)], [tile(i) for i in (41, 42, 43, 24)],
                       [tile(i) for i in (4, 5, 6, 7)], [tile(21), tile(12)], [tile(22), tile(23)]),
               "rwkv": ([tile(33), tile(34)], [tile(41), tile(42)], [tile(43), H[:, 0, :]],
                        [H[:, 1, :], H[:, 2, :]], [H[:, 3, :], tile(40)])}
        RT = {"a": tile(22), "v": tile(23), "bd": tile(12), "kd": tile(32), "z": tile(35), "w": tile(40),
              "aak": [tile(35), tile(40)], "rb": [tile(33), tile(34)], "rk": [tile(41), tile(42)]}

        block = ctx.enter_context(nc.Block())

        @block.sync
        def _(sp):
            sp.dma_start(CST[:], cst_in).then_inc(consts_in, 16)
            sp.dma_start(VEC[:], vec_in).then_inc(consts_in, 16)
            sp.dma_start(X[:], x_in).then_inc(consts_in, 16)
            sp.dma_start(SMALL[:], small_in).then_inc(consts_in, 16)

            wk_v, wd_v = w_k.rearrange("u p n -> p u n"), w_d.rearrange("u p n -> p u n")

            def load(name, j, i=None):
                u = UNIT0[name] + j
                kind = dict((n, k) for n, _, k in STREAM)[name]
                src, width = (wk_v, UNIT) if kind == "k" else (wd_v, UNIT_D)
                at = IN_ARRAY[name] + j
                if u >= SLOTS:
                    sp.wait_ge(unit_used, u - SLOTS + 1 if i is None else i * SLOTS + (u - SLOTS + 1))
                where = at if i is None else i * SLOTS + at
                sp.dma_start(RING[:, u % SLOTS:u % SLOTS + 1, 0:width],
                             src[:, bass.ds(where, 1), :]).then_inc(w_loaded[u % SLOTS], 16)

            for name, count, _ in STREAM:
                peeled = SLOTS if name == "ada0" else 0
                for j in range(peeled):
                    load(name, j)
                groups = (count - peeled) // SLOTS
                with sp.Fori(0, groups, 1) as i:
                    for j in range(SLOTS):
                        load(name, peeled + j, i)
                for j in range(peeled + groups * SLOTS, count):
                    load(name, j)
                if name in ("first0", "first1"):
                    sp.wait_ge(*dve_done("ln", int(name[-1])))
                    sp.dma_start(BIG[:, 34:42, :], dft_in).then_inc(dft_in_s, 16)
            sp.wait_ge(*dve_done("x", "end"))
            sp.dma_start(out, X[:]).then_inc(out_stored, 16)
            sp.wait_ge(out_stored, 16)

        @block.tensor
        def _(pe):
            def mm(o, lhsT, rhs, start=True, stop=True):
                return pe.matmul(o, lhsT, rhs, start=start, stop=stop, skip_group_check=True)

            def step(ins, *name):
                ins.then_inc(*pe_signal(name if len(name) > 1 else name[0]))

            def drain(ins):
                ins.then_inc(*pe_signal())
                pe.wait_ge(*pe_so_far())

            def modulation(layer):
                name = f"ada{layer}"
                with pe.Fori(0, 24 // SLOTS, 1) as i:
                    for j in range(SLOTS):
                        pe.wait_ge(*loaded(UNIT0[name] + j, i))
                        for k in range(KT):
                            ins = mm(PS[7][:, bass.ds(i * SLOTS + (24 * layer + j), 1)],
                                     RING[:, (UNIT0[name] + j) % SLOTS, col(k)], v("c", k),
                                     start=(k == 0), stop=(k == KT - 1))
                        ins.then_inc(unit_used, 1)

            def project(name):
                def unit(j, i, is_tm):
                    u, c = UNIT0[name] + j, COPIED[name] + j
                    pe.wait_ge(*loaded(u, i))
                    if c >= 4:
                        pe.wait_ge(tile_copied, c - 3 if i is None else i * SLOTS + (c - 3))
                    w, bank = RING[:, u % SLOTS, :], PS[c % 4]
                    if is_tm:
                        for tt in range(TT):
                            for k in range(KT):
                                ins = mm(bank[:, col(tt)], H[:, k, col(tt)], w[:, col(k)],
                                         start=(k == 0), stop=(k == KT - 1))
                    else:
                        for k in range(KT):
                            ins = mm(bank[:], w[:, col(k)], H[:, k, :], start=(k == 0), stop=(k == KT - 1))
                    ins.then_inc(unit_used, 1)

                for at, groups, width, is_tm in segments(name):
                    if groups > 1:
                        with pe.Fori(0, groups, 1) as i:
                            for j in range(width):
                                unit(at + j, i, is_tm)
                    else:
                        for j in range(width):
                            unit(at + j, None, is_tm)

            def mean_over_features(norm, what, source, bank, after):
                for k in range(KT):
                    pe.wait_ge(*after(k))
                    ins = mm(bank[:], cst("onesD"), source(k), start=(k == 0), stop=(k == KT - 1))
                step(ins, what, norm)

            def mean_square(norm):
                mean_over_features(norm, "ms", lambda k: BIG[:, 36 + k, :], PS[7], lambda k: act_done("sq", norm, k))

            def layer_norm(norm, after):
                mean_over_features(norm, "mean", lambda k: X[:, k, :], PS[6], lambda k: after)
                mean_square(norm)

            def rope_and_attention(l):
                for t in range(5):
                    pe.wait_ge(*act_done("rsq", l, t))
                    step(mm(PS[t][:], cst("blk64"), tile(22 + t)), "rms", l, t)
                for t in range(5):
                    pe.wait_ge(*dve_done("rn", l, t))
                    step(mm(PS[t][:], cst("perm"), tile(t)), "rot", l, t)

                def scores(w):
                    hh, qt = w // 4, w % 4
                    t, s = hh // 2, 64 * (hh % 2)
                    if w == 0:
                        pe.wait_ge(*dve_done("rope", l, 4))
                    if w >= 2:
                        pe.wait_ge(*act_done("exp", l, w - 2))
                    step(mm(PS[w % 2][:], tile(Q0 + t)[s:s + 64, col(qt)], tile(K0)[s:s + 64, :]), "score", l, w)

                def turn(w):
                    hh, qt = w // 4, w % 4
                    pe.wait_ge(*dve_done("probs", l, w))
                    if w >= 2:
                        pe.wait_ge(*act_done("pT", l, w - 2))
                    for st in range(TT):
                        ins = pe.transpose(PS[2 + w % 2][:, col(st)], tile(22 + w % 2)[:, col(st)], cst("ident"))
                    step(ins, "turned", l, w)

                def values(hh):
                    t, s, pt = hh // 2, 64 * (hh % 2), 24 + 4 * (hh % 2)
                    pe.wait_ge(*act_done("pT", l, 4 * hh + 3))
                    if t >= 2 and s == 0:
                        pe.wait_ge(*dve_done("yattn", l, t - 2))
                    for st in range(TT):
                        ins = mm(PS[4 + t % 2][s:s + 64, :], tile(V0)[:, st * P + s:st * P + s + 64],
                                 tile(pt + st), start=(st == 0), stop=(st == TT - 1))
                    step(ins, "attn", l, hh)

                for w in range(34):
                    if w < 32:
                        scores(w)
                    if 1 <= w <= 32:
                        turn(w - 1)
                    if w >= 2 and (w - 2) % 4 == 3:
                        values((w - 2) // 4)

            def fourier(l):
                pe.wait_ge(consts_in, 64)
                fm = SMALL[:, SCOL["fmix"] + l * 2 * P:SCOL["fmix"] + (l + 1) * 2 * P]
                pe.wait_ge(*dve_done("yattn", l, 3))
                mm(PS[6][:, 0:2 * P], cst("c64"), fm)
                step(mm(PS[6][:, 2 * P:4 * P], cst("s64"), fm), "fmix", l)
                pe.wait_ge(*act_done("fmix", l))
                cm = tile(24).rearrange("p (a c) -> p a c", a=2)
                for tt in range(TT):
                    for j in range(2):
                        ins = mm(PS[tt].rearrange("p (a c) -> p a c", a=2)[:, :, j * P:(j + 1) * P],
                                 tile(FU0 + j)[:, col(tt)], cm[:, :, j * P:(j + 1) * P])
                    step(ins, "ft", l, tt)
                pe.wait_ge(dft_in_s, 16 * (l + 1))
                for j in range(2):
                    for tt in range(TT):
                        pe.wait_ge(*act_done("ft", l, tt))
                        mm(PS[4 + j][:], tile(25 + tt)[:, j * P:(j + 1) * P], tile(34 + tt), start=(tt == 0), stop=False)
                        ins = mm(PS[4 + j][:], tile(25 + tt)[:, (2 + j) * P:(3 + j) * P], tile(38 + tt),
                                 start=False, stop=(tt == TT - 1))
                    step(ins, "four", l, j)

            def ffn(f):
                up, down = f"ffn{f}", f"down{f}"
                pe.wait_ge(*dve_done("h", f))
                with pe.Fori(0, FT // 2, 1) as i:
                    for j in range(2):
                        for w, evacuated in ((0, act_done("silu", f, j, i=i, lag=1)),
                                             (1, dve_done("gated", f, j, i=i, lag=1))):
                            u = UNIT0[up] + 2 * j + w
                            pe.wait_ge(*loaded(u, i))
                            pe.wait_ge(*evacuated)
                            for k in range(KT):
                                ins = mm(PS[2 * j + w][:], RING[:, u % SLOTS, col(k)], H[:, k, :],
                                         start=(k == 0), stop=(k == KT - 1))
                            ins.then_inc(unit_used, 1)
                pe.wait_ge(*dve_done("gated", f, 1))
                with pe.Fori(0, KT // 2, 1) as i:
                    for j in range(2):
                        pe.wait_ge(*act_done("downed", f, j, i=i, lag=1))
                        for half in range(2):
                            u = UNIT0[down] + 2 * j + half
                            pe.wait_ge(*loaded(u, i))
                            for k in range(KD):
                                ins = mm(PS[4 + j][:], RING[:, u % SLOTS, col(k)], tile(half * KD + k),
                                         start=(half == k == 0), stop=(half == 1 and k == KD - 1))
                            ins.then_inc(unit_used, 1)
                mean_square(("post", f))

            def head_norms(m):
                for h in range(4):
                    pe.wait_ge(*act_done("hsq", m, h))
                    step(mm(PS[h][:], cst("ones128"), tile(HSQ[m][h])), "hms", m, h)

            def invert(m):
                lt, xs, xts, nts, ps = INV[m[0]]
                n = LEVELS * len(lt)

                def nx(q):
                    pe.wait_ge(*dve_done("nT", m, q))
                    for tt in range(TT):
                        ins = mm(PS[3 * (q % 2)][:, col(tt)], nts[q % 2][:, col(tt)], xs[q % len(lt)][:, col(tt)])
                    step(ins, "nx", m, q)

                nx(0)
                for q in range(n):
                    if q + 1 < n:
                        nx(q + 1)
                    h, bank = q % len(lt), 3 * (q % 2)
                    pe.wait_ge(*act_done("nx", m, q))
                    if q < n - len(lt):
                        for tt in range(TT):
                            mm(PS[bank + 1][:, col(tt)], xts[h][:, col(tt)], ps[q % 2][:, col(tt)])
                    for tt in range(TT):
                        ins = mm(PS[bank + 2][:, col(tt)], ps[q % 2][:, col(tt)], xts[h][:, col(tt)])
                    step(ins, "xnx", m, q)

            def linear_attention():
                m = "gla"
                pe.wait_ge(tile_copied, COPIED["mix0"] + N_EVEN)
                for j in range(2):
                    step(mm(PS[j][:], SMALL[0:16, SCOL["lora"] + j * P:SCOL["lora"] + (j + 1) * P],
                            tile(SM0)[0:16, :]), "gate", j)
                for j in range(2):
                    pe.wait_ge(*dve_done("kdec", j))
                    for tt in range(TT):
                        ins = pe.transpose(PS[2 + j][:, col(tt)], tile(33 + j)[:, col(tt)], cst("ident"))
                    step(ins, "kdT", j)
                for j in range(2):
                    pe.wait_ge(*act_done("kdT", j))
                    for odd in range(2):
                        for c in range(odd, NCH - 1, 2):
                            r, tt = CH * odd, c // 2
                            for s in range(2):
                                ins = mm(PS[4 + 2 * j + c // 4][CH * s:CH * s + CH, col(c % 4)],
                                         tile(31 + j)[r:r + CH, tt * P + CH * s:tt * P + CH * s + CH],
                                         tile(GV0 + 2 * j + s)[r:r + CH, col(tt)])
                        if not odd:
                            drain(ins)
                    step(ins, "kv", j)
                pe.wait_ge(*dve_done("kn", 1))
                for h in range(4):
                    j, s = h // 2, CH * (h % 2)
                    for tt in range(TT):
                        ins = mm(PS[h][:, col(tt)], tile(GK0 + j)[s:s + CH, col(tt)], tile(GQ0 + j)[s:s + CH, col(tt)])
                    step(ins, "gatt", h)
                pe.wait_ge(*dve_done("states"))
                for h in range(4):
                    j, s = h // 2, CH * (h % 2)
                    pe.wait_ge(*dve_done("gatt", h))
                    for tt in range(TT):
                        mm(PS[4 + h][:, col(tt)], tile(GV0 + h)[:, col(tt)], tile(GATT[h])[:, col(tt)],
                           start=(tt == 0), stop=False)
                    for c in range(1, NCH):
                        ins = mm(PS[4 + h][:, col(c, CH)], gla_state(j, c)[s:s + CH, :],
                                 tile(GQ0 + j)[s:s + CH, col(c, CH)], start=False, stop=(c == NCH - 1))
                    step(ins, "o", m, h)
                head_norms(m)

            def delta_rule():
                m = "gdn"
                pe.wait_ge(*dve_done("yh", "gla", 3))
                for t in range(8):
                    pe.wait_ge(*act_done("l2sq", t))
                    step(mm(PS[t][:], cst("ones1"), tile(13 + t)), "l2", t)
                pe.wait_ge(*act_done("rows"))
                pe.wait_ge(*dve_done("l2n", 7))
                for tt in range(TT):
                    ins = pe.transpose(PS[0][:, col(tt)], tile(22)[:, col(tt)], cst("ident"))
                step(ins, "cols")
                pe.wait_ge(*act_done("cols"))
                for h in range(4):
                    mm(PS[h][:], cst("sel", h * P, h * P + P)[DA_ROW:DA_ROW + 4, :], tile(22)[DA_ROW:DA_ROW + 4, :])
                    step(mm(PS[4 + h][:], cst("sel", h * P, h * P + P)[DB_ROW:DB_ROW + 4, :],
                            tile(22)[DB_ROW:DB_ROW + 4, :]), "rowb", h)
                for h in range(4):
                    pe.wait_ge(*dve_done("kb", h))
                    pe.wait_ge(*act_done("egb", h))
                    for tt in range(TT):
                        mm(PS[h][:, col(tt)], tile(4 + h)[:, col(tt)], tile(h)[:, col(tt)])
                    for tt in range(TT):
                        ins = mm(PS[4 + h][:, col(tt)], tile(4 + h)[:, col(tt)], tile(37 + h)[:, col(tt)])
                    step(ins, "datt", h)
                for h in range(4):
                    pe.wait_ge(*dve_done("dLT", h))
                    for tt in range(TT):
                        pe.transpose(PS[h][:, col(tt)], tile(4 + h)[:, col(tt)], cst("ident"))
                    for tt in range(TT):
                        ins = pe.transpose(PS[4 + h][:, col(tt)], tile(8 + h)[:, col(tt)], cst("ident"))
                    step(ins, "dtok", h)
                for h in range(4):
                    pe.wait_ge(*act_done("dtok", h))
                invert((m, 0))
                pe.wait_ge(*dve_done("inv", (m, 0)))
                for tt in range(TT):
                    for h in range(4):
                        ins = mm(PS[tt][:, col(h)], INV[m][2][h][:, col(tt)], tile(8 + h)[:, col(tt)])
                    step(ins, "du", tt)
                for h in range(4):
                    for tt in range(TT):
                        ins = mm(PS[4 + h][:, col(tt)], tile(37 + h)[:, col(tt)], INV[m][2][h][:, col(tt)])
                    step(ins, "dw", h)
                pe.wait_ge(*act_done("dw", 3))
                pe.wait_ge(*act_done("du", 3))
                for c in range(NCH):
                    r, tt = CH * (c % 2), c // 2
                    if c:
                        pe.wait_ge(*dve_done("dstate", c - 1))
                        for h in range(4):
                            ins = mm(PS[0][:, col(h)], INV[m][1][h][:, col(tt)], STATE[:, col(h)])
                        step(ins, "dws", c)
                        for h in range(4):
                            mm(PS[4 + h][:, col(c, CH)], STATE[:, col(h)], tile(13 + h)[:, col(c, CH)],
                               start=(c == 1), stop=False)
                    pe.wait_ge(*dve_done("dv", c))
                    if c < NCH - 1:
                        for h in range(4):
                            ins = mm(PS[1][:, col(h)], tile(29 + h)[r:r + CH, col(tt)], tile(8 + tt)[r:r + CH, col(h)])
                        step(ins, "dupd", c)
                    if c % 2:
                        for h in range(4):
                            ins = mm(PS[4 + h][:, col(tt)], tile(8 + tt)[:, col(h)], tile(h)[:, col(tt)],
                                     start=False, stop=(tt == TT - 1))
                            if tt == TT - 1:
                                step(ins, "o", m, h)
                head_norms(m)

            def lru():
                for j in range(4):
                    pe.wait_ge(*dve_done("lconv", j))
                    mm(PS[j][:], SMALL[:, SCOL["lwa"] + j * P:SCOL["lwa"] + (j + 1) * P], tile(22 + j))
                    step(mm(PS[4 + j][:], SMALL[:, SCOL["lwx"] + j * P:SCOL["lwx"] + (j + 1) * P], tile(22 + j)),
                         "lgate", j)

            def rwkv():
                pe.wait_ge(*act_done("rlora"))
                pe.wait_ge(*act_done("lgate", 3))
                wa2 = SMALL[:, SCOL["wa2"]:SCOL["wa2"] + 4 * P]
                for j in range(4):
                    mm(PS[j][:], wa2[0:64, col(j)], tile(WA0)[0:64, :])
                    step(mm(PS[4 + j][:], wa2[64:128, col(j)], tile(WA0)[64:128, :]), "rlora", j)
                for j in range(4):
                    pe.wait_ge(*act_done("kksq", j))
                    step(mm(PS[j][:], cst("blk1"), tile(40 + j)), "kk2", j)
                for j in range(4):
                    pe.wait_ge(*dve_done("bonus0", j))
                    step(mm(PS[4 + j][:], cst("blk1"), tile(14 + j)), "bonus", j)
                pe.wait_ge(*dve_done("rprep"))
                for tt in range(TT):
                    m = ("rwkv", tt)
                    if tt:
                        pe.wait_ge(*act_done("ry", tt - 1))
                        pe.wait_ge(*dve_done("rstate", 2 * tt - 1))
                    for q in range(4):
                        for j in range(4):
                            ins = pe.transpose(PS[q][:, col(j)], tile((24, 8, 28, 18)[q] + j)[:, col(tt)], cst("ident"))
                        step(ins, "rtok", tt, q)

                    def pairs(bank, left, right):
                        for h in range(8):
                            j, s = h // 2, 64 * (h % 2)
                            ins = mm(PS[bank + h % 2][:, col(j)], tile(left + j)[s:s + 64, col(tt)],
                                     tile(right + j)[s:s + 64, col(tt)])
                        return ins

                    pairs(4, 36, 24)
                    step(pairs(6, 4, 24), "rmat", tt)
                    pe.wait_ge(*dve_done("rmat", tt))
                    for q in range(4):
                        pe.wait_ge(*act_done("rtok", tt, q))
                    for h in range(8):
                        ins = mm(PS[0][:, col(h, 64)], RT["aak"][h % 2][:, col(h // 2)], RT["v"][:, col(h, 64)])
                    step(ins, "rz", tt)
                    pe.wait_ge(*act_done("rz", tt))
                    invert(m)
                    pe.wait_ge(*dve_done("inv", m))
                    xt = INV["rwkv"][2]
                    for h in range(8):
                        ins = mm(PS[0][:, col(h, 64)], xt[h % 2][:, col(h // 2)], RT["z"][:, col(h, 64)])
                    step(ins, "ru", tt)
                    for h in range(8):
                        j, s = h // 2, 64 * (h % 2)
                        ins = mm(PS[1][s:s + 64, col(j)], RT["a"][:, col(h, 64)], xt[h % 2][:, col(h // 2)])
                    step(ins, "rw", tt)
                    pairs(4, 36, 0)
                    step(pairs(6, 4, 0), "rout", tt)
                    pe.wait_ge(*act_done("rw", tt))
                    pe.wait_ge(*dve_done("rout", tt))
                    started = set()
                    for c in (2 * tt, 2 * tt + 1):
                        r = CH * (c % 2)
                        if c:
                            pe.wait_ge(*dve_done("rstate", c - 1))
                            for h in (0, 2, 4, 6, 1, 3, 5, 7):
                                j, s = h // 2, 64 * (h % 2)
                                ins = mm(PS[3][:, col(h, 64)], RT["w"][s:s + 64, col(j)], STATE[s:s + 64, col(j, 64)])
                                if h == 6:
                                    drain(ins)
                            step(ins, "rws", c)
                            for h in (1, 3, 5, 7, 0, 2, 4, 6):
                                j, s = h // 2, 64 * (h % 2)
                                mm(PS[2][s:s + 64, j * P + r:j * P + r + CH], STATE[s:s + 64, col(j, 64)],
                                   tile(j)[s:s + 64, col(c, CH)], start=(s not in started), stop=False)
                                started.add(s)
                        pe.wait_ge(*dve_done("ruc", c))
                        if c < NCH - 1:
                            for h in range(8):
                                j, s = h // 2, 64 * (h % 2)
                                mm(PS[1][s:s + 64, col(j, 64)], RT["bd"][r:r + CH, col(h, 64)],
                                   RT["z"][r:r + CH, col(h, 64)], start=True, stop=False)
                                ins = mm(PS[1][s:s + 64, col(j, 64)], RT["kd"][r:r + CH, col(h, 64)],
                                         RT["v"][r:r + CH, col(h, 64)], start=False, stop=True)
                            step(ins, "rupd", c)
                    for h in range(8):
                        j, s = h // 2, 64 * (h % 2)
                        mm(PS[2][s:s + 64, col(j)], RT["z"][:, col(h, 64)], RT["rb"][h % 2][:, col(h // 2)],
                           start=False, stop=False)
                        ins = mm(PS[2][s:s + 64, col(j)], RT["v"][:, col(h, 64)], RT["rk"][h % 2][:, col(h // 2)],
                                 start=False, stop=True)
                    step(ins, "ry", tt)
                pe.wait_ge(*act_done("ry", TT - 1))
                for j in range(4):
                    step(mm(PS[j][:], cst("blk64"), tile(j)), "gmean", j)
                for j in range(4):
                    pe.wait_ge(*act_done("gsq", j))
                    step(mm(PS[4 + j][:], cst("blk64"), tile(22 + j)), "gvar", j)
                for j in range(4):
                    pe.wait_ge(*dve_done("gcentred", j))
                    step(mm(PS[j][:], SMALL[:, SCOL["g2"] + j * P:SCOL["g2"] + (j + 1) * P], tile(GL0)), "gout", j)

            pe.wait_ge(consts_in, 64)
            for l in range(DEPTH):
                modulation(l)
            for l in range(DEPTH):
                layer_norm(("ln", l), dve_done("x", "first", l - 1) if l else (consts_in, 64))
                pe.wait_ge(*dve_done("ln", l))
                project(f"first{l}")
                rope_and_attention(l)
                fourier(l)
                pe.wait_ge(*dve_done("y", "first", l))
                project(f"firstout{l}")
                layer_norm(("pln", l), dve_done("res", l))
            for i in range(DEPTH):
                mean_square(("pre", f"{i}0"))
                ffn(f"{i}0")
                mean_square(("pre", f"mix{i}"))
                pe.wait_ge(*dve_done("h", f"mix{i}"))
                project(f"mix{i}")
                if i % 2 == 0:
                    linear_attention()
                    delta_rule()
                else:
                    lru()
                    rwkv()
                pe.wait_ge(*dve_done("y", "mix", i))
                project(f"mixout{i}")
                mean_square(("post", f"mix{i}"))
                mean_square(("pre", f"{i}1"))
                ffn(f"{i}1")

        @block.scalar
        def _(act):
            def a(o, i, func, *name, bias=0.0, scale=1.0, chain=True, accum=None):
                extra = {} if accum is None else {"accum_out": accum}
                ins = nc.scalar.activation(o, i, func, bias=bias, scale=scale, **extra)
                ins.then_inc(*act_signal((name if len(name) > 1 else name[0]) if name else None))
                if chain:
                    act.wait_ge(*act_so_far())

            def squares(norm, source, after):
                for k in range(KT):
                    act.wait_ge(*after(k))
                    a(BIG[:, 36 + k, :], source(k), ACT.Square, "sq", norm, k, chain=False)
                act.wait_ge(*pe_done("ms", norm))
                a(RSTD[:, 0, :], PS[7][:], ACT.Sqrt, "sd", norm, bias=v("eps5" if norm[0] in ("ln", "pln") else "eps6"))

            def project(name, dest):
                def unit(j, i):
                    c = COPIED[name] + j
                    u = UNIT0[name] + j + 1
                    act.wait_ge(unit_used, u if i is None else i * SLOTS + u)
                    at = dest + j if i is None else i * SLOTS + (dest + j)
                    nc.scalar.activation(BIG[:, bass.ds(at, 1), :], PS[c % 4][:].unsqueeze(1),
                                         ACT.Copy).then_inc(tile_copied, 1)

                for at, groups, width, _ in segments(name):
                    if groups > 1:
                        with act.Fori(0, groups, 1) as i:
                            for j in range(width):
                                unit(at + j, i)
                    else:
                        for j in range(width):
                            unit(at + j, None)
                count = dict((n, c) for n, c, _ in STREAM)[name]
                act.wait_ge(tile_copied, COPIED[name] + count)

            def rope_and_attention(l):
                for t in range(5):
                    a(tile(22 + t), tile(t), ACT.Square, "rsq", l, t, chain=False)
                for t in range(5):
                    act.wait_ge(*pe_done("rms", l, t))
                    a(tile(22 + t), PS[t][:], ACT.Sqrt, "rsd", l, t, bias=v("eps6"))
                for t0, n in ((GA0, 4), (GC0, 2), (GF0, 2)):
                    a(BIG[:, t0:t0 + n, :], BIG[:, t0:t0 + n, :], ACT.Silu, "gates", l, t0)
                for w in range(33):
                    if w < 32:
                        act.wait_ge(*dve_done("negmax", l, w))
                        if w >= 2:
                            act.wait_ge(*pe_done("turned", l, w - 2))
                        a(tile(22 + w % 2), PS[w % 2][:], ACT.Exp, "exp", l, w, bias=STAT[:, 1, w:w + 1],
                          scale=0.125, accum=STAT[:, 2, w:w + 1], chain=False)
                    if w:
                        u = w - 1
                        hh = u // 4
                        act.wait_ge(*pe_done("turned", l, u))
                        if hh >= 2:
                            act.wait_ge(*pe_done("attn", l, hh - 2))
                        pt = 24 + 4 * (hh % 2)
                        a(BIG[:, pt:pt + 4, col(u % 4)], by_tt(PS[2 + u % 2][:]), ACT.Copy, "pT", l, u, chain=False)

            def fourier(l):
                act.wait_ge(*pe_done("fmix", l))
                a(tile(24), PS[6][:], ACT.Copy, "fmix", l, chain=False)
                for tt in range(TT):
                    act.wait_ge(*pe_done("ft", l, tt))
                    a(tile(25 + tt), PS[tt][:], ACT.Copy, "ft", l, tt, chain=False)

            def ffn(f):
                up, down = UNIT0[f"ffn{f}"], UNIT0[f"down{f}"]
                first = act_begin_loop()
                with act.Fori(0, FT // 2, 1) as i:
                    for j in range(2):
                        act.wait_ge(unit_used, i * SLOTS + (up + 2 * j + 1))
                        act.wait_ge(*dve_done("gated", f, j, i=i, lag=1))
                        a(GATE[:, j, :], PS[2 * j][:], ACT.Silu, "silu", f, j, chain=False)
                act_end_loop(first, FT // 2)
                first = act_begin_loop()
                with act.Fori(0, KT // 2, 1) as i:
                    for j in range(2):
                        act.wait_ge(unit_used, i * SLOTS + (down + 2 * j + 2))
                        a(H[:, bass.ds(i * 2 + j, 1), :], PS[4 + j][:].unsqueeze(1), ACT.Copy, "downed", f, j,
                          chain=False)
                act_end_loop(first, KT // 2)
                squares(("post", f), lambda k: H[:, k, :], lambda k: act_done("downed", f, 1))

            def head_norms(m, bank):
                for h in range(4):
                    act.wait_ge(*pe_done("o", m, h))
                    a(tile(HSQ[m][h]), PS[bank + h][:], ACT.Square, "hsq", m, h, chain=False)
                for h in range(4):
                    act.wait_ge(*pe_done("hms", m, h))
                    a(tile(HSQ[m][h]), PS[h][:], ACT.Sqrt, "hsd", m, h, bias=v("eps6"), chain=False)

            def invert(m):
                lt, _, _, _, ps = INV[m[0]]
                for q in range(LEVELS * len(lt)):
                    act.wait_ge(*pe_done("nx", m, q))
                    a(ps[q % 2], PS[3 * (q % 2)][:], ACT.Copy, "nx", m, q, chain=False)

            def softplus_part(o, x):
                a(o, x, ACT.Abs)
                a(o, o, ACT.Exp, scale=-1.0)

            def linear_attention():
                for j in range(2):
                    act.wait_ge(*pe_done("gate", j))
                    a(tile(29 + j), PS[j][:], ACT.Identity, bias=v("lorab", j))
                    softplus_part(tile(31 + j), tile(29 + j))
                for j in range(2):
                    a(tile(31 + j), tile(31 + j), ACT.Ln, "lsig", j, bias=v("one"))
                for j in range(2):
                    act.wait_ge(*dve_done("dl", j))
                    a(tile(35 + j), tile(31 + j), ACT.Exp, scale=1 / 16)
                    a(tile(29 + j), tile(31 + j), ACT.Exp, scale=-1 / 16)
                    a(tile(33 + j), tile(33 + j), ACT.Exp, "gexp", j, scale=1 / 16)
                a(BIG[:, GG0:GG0 + 4, :], BIG[:, GG0:GG0 + 4, :], ACT.Silu, "ggate")
                for j in range(2):
                    act.wait_ge(*pe_done("kdT", j))
                    a(tile(31 + j), PS[2 + j][:], ACT.Copy, "kdT", j)
                head_norms("gla", 4)

            def delta_rule():
                for t in range(12):
                    act.wait_ge(*dve_done("dconv", t))
                    a(tile(t), tile(t), ACT.Silu, "dconv", t)
                a(BIG[:, DZ0:DZ0 + 4, :], BIG[:, DZ0:DZ0 + 4, :], ACT.Silu, "zgate")
                for t in range(8):
                    a(tile(13 + t), tile(t), ACT.Square, "l2sq", t, chain=False)
                g, b = slice(DA_ROW, DA_ROW + 4), slice(DB_ROW, DB_ROW + 4)
                a(tile(SM0)[g], tile(SM0)[g], ACT.Identity, bias=v("dtb")[g])
                softplus_part(tile(21)[g], tile(SM0)[g])
                a(STAT[g, 0, 0:1], v("alog")[g], ACT.Exp)
                a(tile(21)[g], tile(21)[g], ACT.Ln, "dsp", bias=v("one")[g])
                act.wait_ge(*dve_done("rows0"))
                a(tile(22)[b], tile(SM0)[b], ACT.Sigmoid, "beta")
                for t in range(8):
                    act.wait_ge(*pe_done("l2", t))
                    a(tile(13 + t), PS[t][:], ACT.Sqrt, "l2sd", t, bias=v("eps6"), chain=False)
                act.wait_ge(*dve_done("gc"))
                a(tile(22)[EG_ROW:EG_ROW + 4], tile(22)[g], ACT.Exp)
                e = slice(ED_ROW, ED_ROW + 4)
                a(tile(22)[e], tile(22)[e], ACT.Exp, "rows")
                act.wait_ge(*pe_done("cols"))
                a(tile(23), PS[0][:], ACT.Copy, "cols")
                for h in range(4):
                    act.wait_ge(*pe_done("rowb", h))
                    a(tile(33 + h), PS[h][:], ACT.Exp, "egb", h, chain=False)
                    act.wait_ge(*dve_done("ddec", h))
                    a(tile(29 + h), tile(29 + h), ACT.Exp, "ddec", h)
                act.wait_ge(*dve_done("colbe"))
                for h in range(4):
                    act.wait_ge(*pe_done("dtok", h))
                    for tt in range(TT):
                        c = tt * P + h
                        cols = tile(23)
                        a(tile(37 + h)[:, col(tt)], PS[h][:, col(tt)], ACT.Copy, scale=STAT[:, 1, 4 * tt + h:4 * tt + h + 1],
                          chain=False)
                        a(tile(29 + h)[:, col(tt)], PS[h][:, col(tt)], ACT.Copy,
                          scale=cols[:, c + ED_ROW:c + ED_ROW + 1], chain=False)
                    for tt in range(TT):
                        c = tt * P + h
                        last = dict(chain=False)
                        name = ("dtok", h) if tt == TT - 1 else ()
                        a(tile(8 + h)[:, col(tt)], PS[4 + h][:, col(tt)], ACT.Copy, *name,
                          scale=tile(23)[:, c + DB_ROW:c + DB_ROW + 1], **last)
                invert(("gdn", 0))
                for tt in range(TT):
                    act.wait_ge(*pe_done("du", tt))
                    a(tile(17 + tt), PS[tt][:], ACT.Copy, "du", tt, chain=False)
                for h in range(4):
                    act.wait_ge(*pe_done("dw", h))
                    a(INV["gdn"][1][h], PS[4 + h][:], ACT.Copy, "dw", h, chain=False)
                head_norms("gdn", 4)

            def lru():
                act.wait_ge(consts_in, 64)
                a(LRUV[:, 0:4], v4("lam"), ACT.Abs)
                a(LRUV[:, 0:4], LRUV[:, 0:4], ACT.Exp, "lam", scale=-1.0)
                for j in range(4):
                    act.wait_ge(*pe_done("lgate", j))
                    a(tile(26 + j), PS[j][:], ACT.Sigmoid, bias=v("lba", j), chain=False)
                    a(tile(30 + j), PS[4 + j][:], ACT.Sigmoid, "lgate", j, bias=v("lbx", j))
                act.wait_ge(*dve_done("lam"))
                for j in range(4):
                    a(tile(34 + j), tile(26 + j), ACT.Exp, scale=LRUV[:, 8 + j:9 + j], chain=False)
                    a(tile(26 + j), tile(26 + j), ACT.Tanh, "ltanh", j, scale=LRUV[:, 12 + j:13 + j])
                for j in range(4):
                    act.wait_ge(*dve_done("gelu0", j))
                    a(tile(14 + j), tile(14 + j), ACT.Tanh, "gelu", j, scale=float(np.sqrt(2 / np.pi)), chain=False)
                for j in range(4):
                    act.wait_ge(*dve_done("lmult", j))
                    a(tile(38 + j), tile(38 + j), ACT.Sqrt, "lmult", j, chain=False)

            def rwkv():
                act.wait_ge(*dve_done("shift", WA0))
                a(tile(WA0)[0:64], tile(WA0)[0:64], ACT.Tanh)
                act.wait_ge(*dve_done("shift", GL0))
                a(tile(GL0), tile(GL0), ACT.Sigmoid, "rlora")
                act.wait_ge(*dve_done("shift", WA0 - 1))
                for j in range(4):
                    act.wait_ge(*pe_done("rlora", j))
                    a(tile(24 + j), PS[j][:], ACT.Sigmoid, bias=v("w0", j), chain=False)
                    a(tile(28 + j), PS[4 + j][:], ACT.Sigmoid, "rgate", j, bias=v("a0", j), chain=False)
                for j in range(4):
                    act.wait_ge(*dve_done("kk", j))
                    a(tile(40 + j), tile(36 + j), ACT.Square, "kksq", j, chain=False)
                for j in range(4):
                    act.wait_ge(*pe_done("kk2", j))
                    a(tile(40 + j), PS[j][:], ACT.Sqrt, "kksd", j, bias=v("eps6"), chain=False)
                for j in range(4):
                    act.wait_ge(*dve_done("rcum", j))
                    a(tile(24 + j), tile(24 + j), ACT.Exp, scale=-DECAY, chain=False)
                    a(tile(32 + j), tile(40 + j), ACT.Exp, scale=-DECAY)
                    a(tile(40 + j), tile(40 + j), ACT.Exp, scale=DECAY, chain=False)
                    a(tile(18 + j), tile(18 + j), ACT.Exp, "rexp", j, scale=-DECAY, chain=False)
                for tt in range(TT):
                    m = ("rwkv", tt)
                    for q, name in enumerate(("a", "v", "bd", "kd")):
                        act.wait_ge(*pe_done("rtok", tt, q))
                        a(RT[name], PS[q][:], ACT.Copy, "rtok", tt, q, chain=False)
                    act.wait_ge(*pe_done("rz", tt))
                    a(RT["z"], PS[0][:], ACT.Copy, "rz", tt)
                    invert(m)
                    act.wait_ge(*pe_done("ru", tt))
                    a(RT["z"], PS[0][:], ACT.Copy, "ru", tt)
                    act.wait_ge(*pe_done("rw", tt))
                    a(RT["w"], PS[1][:], ACT.Copy, "rw", tt)
                    act.wait_ge(*pe_done("ry", tt))
                    a(BIG[:, 0:4, col(tt)], by_tt(PS[2][:]), ACT.Copy, "ry", tt)
                for j in range(4):
                    act.wait_ge(*dve_done("gcentred", j))
                    a(tile(22 + j), tile(j), ACT.Square, "gsq", j, chain=False)
                for j in range(4):
                    act.wait_ge(*pe_done("gvar", j))
                    a(tile(22 + j), PS[4 + j][:], ACT.Sqrt, "gsd", j, bias=v("epsg"), chain=False)

            act.wait_ge(consts_in, 64)
            for l in range(DEPTH):
                squares(("ln", l), lambda k: H[:, k, :], lambda k: dve_done("xc", ("ln", l), k))
                project(f"first{l}", 0)
                rope_and_attention(l)
                fourier(l)
                project(f"firstout{l}", 0)
                squares(("pln", l), lambda k: H[:, k, :], lambda k: dve_done("xc", ("pln", l), k))
            for i in range(DEPTH):
                ready = dve_done("x", "first", 1) if i == 0 else dve_done("x", "11" if i == 2 else "01")
                squares(("pre", f"{i}0"), lambda k: X[:, k, :], lambda k: ready)
                ffn(f"{i}0")
                squares(("pre", f"mix{i}"), lambda k: X[:, k, :], lambda k: dve_done("x", f"{i}0"))
                project(f"mix{i}", 0)
                if i % 2 == 0:
                    linear_attention()
                    delta_rule()
                else:
                    lru()
                    rwkv()
                project(f"mixout{i}", 0)
                squares(("post", f"mix{i}"), lambda k: tile(k), lambda k: (tile_copied, COPIED[f"mixout{i}"] + KT))
                squares(("pre", f"{i}1"), lambda k: X[:, k, :], lambda k: dve_done("x", f"mix{i}"))
                ffn(f"{i}1")

        @block.vector
        def _(dve):
            ve = nc.vector

            def d(ins, *name, chain=True):
                ins.then_inc(*dve_signal((name if len(name) > 1 else name[0]) if name else None))
                if chain:
                    dve.wait_ge(*dve_so_far())

            def stt(o, a, s, b, op0, op1):
                return ve.scalar_tensor_tensor(out=o, in0=a, scalar=s, in1=b, op0=op0, op1=op1)

            def reciprocal_std(norm):
                dve.wait_ge(*act_done("sd", norm))
                d(ve.reciprocal(RSTD[:, 1, :], RSTD[:, 0, :]))

            def layer_norm(norm, l, first):
                dve.wait_ge(*pe_done("mean", norm))
                for k in range(KT):
                    d(ve.tensor_tensor(H[:, k, :], X[:, k, :], PS[6][:], ALU.subtract), "xc", norm, k, chain=False)
                reciprocal_std(norm)
                for k in range(KT):
                    if first:
                        d(ve.tensor_tensor(H[:, k, :], H[:, k, :], RSTD[:, 1, :], ALU.mult))
                        d(ve.tensor_scalar(H[:, k, :], H[:, k, :], MOD[:, l, 8 + k:9 + k], MOD[:, l, k:k + 1],
                                           ALU.mult, ALU.add))
                    else:
                        d(stt(X[:, k, :], H[:, k, :], v("lng", 8 * l + k), RSTD[:, 1, :], ALU.mult, ALU.mult))
                        d(ve.tensor_scalar(X[:, k, :], X[:, k, :], v("lnb", 8 * l + k), None, ALU.add),
                          *(("x", "first", l) if k == KT - 1 else ()))
                if first:
                    d(ve.memset(STAT[:, 3, 0:1], 0.0), "ln", l)

            def pre_norm(name, w):
                reciprocal_std(("pre", name))
                for k in range(KT):
                    d(stt(H[:, k, :], X[:, k, :], v("nw", w * 8 + k), RSTD[:, 1, :], ALU.mult, ALU.mult),
                      *(("h", name) if k == KT - 1 else ()), chain=(k == KT - 1))

            def post_norm(name, w, source, factor):
                reciprocal_std(("post", name))
                for k in range(KT):
                    d(stt(source(k), source(k), v("nw", w * 8 + k), RSTD[:, 1, :], ALU.mult, ALU.mult))
                    d(stt(X[:, k, :], source(k), factor, X[:, k, :], ALU.mult, ALU.add),
                      *(("x", name) if k == KT - 1 else ()), chain=(k == KT - 1))

            def modulation():
                dve.wait_ge(consts_in, 64)
                dve.wait_ge(unit_used, UNIT0["first0"])
                d(ve.tensor_tensor(MOD[:].rearrange("p l n -> p (l n)"), PS[7][:, 0:48],
                                   VEC[:, VCOL["bada"]:VCOL["bada"] + 48], ALU.add))
                d(ve.tensor_scalar(MOD[:, :, 8:24], MOD[:, :, 8:24], 1.0, None, ALU.add))

            def rope_and_attention(l):
                dve.wait_ge(tile_copied, COPIED[f"first{l}"] + N_FIRST)
                for t in range(5):
                    dve.wait_ge(*act_done("rsd", l, t))
                    d(ve.reciprocal(tile(22 + t), tile(22 + t)))
                    gain = v("kg", l) if t == K0 else v("qg", l)
                    d(stt(tile(t), tile(t), gain, tile(22 + t), ALU.mult, ALU.mult), "rn", l, t)
                for t in range(5):
                    dve.wait_ge(*pe_done("rot", l, t))
                    d(ve.tensor_tensor(tile(22 + t), PS[t][:], cst("sin"), ALU.mult))
                    d(ve.tensor_tensor(tile(t), tile(t), cst("cos"), ALU.mult))
                    d(ve.tensor_tensor(tile(t), tile(t), tile(22 + t), ALU.add), "rope", l, t)
                for w in range(34):
                    if w < 32:
                        dve.wait_ge(*pe_done("score", l, w))
                        d(ve.reduce_max(STAT[:, 0, w:w + 1], PS[w % 2][:], AX_X))
                        d(ve.tensor_scalar(STAT[:, 1, w:w + 1], STAT[:, 0, w:w + 1], -0.125, None, ALU.mult),
                          "negmax", l, w, chain=False)
                    if 1 <= w <= 32:
                        u = w - 1
                        dve.wait_ge(*act_done("exp", l, u))
                        d(ve.reciprocal(STAT[:, 3, u:u + 1], STAT[:, 2, u:u + 1]))
                        d(ve.tensor_scalar(tile(22 + u % 2), tile(22 + u % 2), STAT[:, 3, u:u + 1], None, ALU.mult),
                          "probs", l, u)
                    if w >= 9 and (w - 9) % 8 == 0 or w == 33:
                        t = (w - 9) // 8
                        if t < 4:
                            dve.wait_ge(*pe_done("attn", l, 2 * t + 1))
                            dve.wait_ge(*act_done("gates", l, GF0))
                            d(ve.tensor_tensor(H[:, t, :], PS[4 + t % 2][:], tile(GA0 + t), ALU.mult), "yattn", l, t)

            def short_conv(l):
                for j in range(2):
                    u, y, w = tile(32 + j), H[:, 4 + j, :], 6 * l + j
                    d(ve.tensor_tensor(u, tile(CC0 + j), tile(CU0 + j), ALU.mult))
                    d(ve.tensor_scalar(y, u, v("cw", w + 2), None, ALU.mult))
                    d(stt(y[:, 1:T], u[:, 0:T - 1], v("cw", w), y[:, 1:T], ALU.mult, ALU.add))
                    d(stt(y[:, 0:T - 1], u[:, 1:T], v("cw", w + 4), y[:, 0:T - 1], ALU.mult, ALU.add))
                    d(ve.tensor_tensor(y, y, tile(CB0 + j), ALU.mult))
                    d(ve.tensor_tensor(y, y, tile(GC0 + j), ALU.mult))

            def residual(l):
                dve.wait_ge(tile_copied, COPIED[f"firstout{l}"] + KT)
                for k in range(KT):
                    d(ve.tensor_scalar(tile(k), tile(k), MOD[:, l, 16 + k:17 + k], None, ALU.mult))
                    d(stt(X[:, k, :], X[:, k, :], ALPHA, tile(k), ALU.mult, ALU.add),
                      *(("res", l) if k == KT - 1 else ()), chain=(k == KT - 1))

            def ffn(f):
                up = UNIT0[f"ffn{f}"]
                first = dve_begin_loop()
                with dve.Fori(0, FT // 2, 1) as i:
                    for j in range(2):
                        dve.wait_ge(*act_done("silu", f, j, i=i))
                        dve.wait_ge(unit_used, i * SLOTS + (up + 2 * j + 2))
                        d(ve.tensor_tensor(BIG[:, bass.ds(i * 2 + j, 1), :], GATE[:, j:j + 1, :],
                                           PS[2 * j + 1][:].unsqueeze(1), ALU.mult), "gated", f, j, chain=False)
                dve_end_loop(first, FT // 2)

            def head_norms(m, bank, y0, gain, gate0):
                for h in range(4):
                    dve.wait_ge(*act_done("hsd", m, h))
                    r = tile(HSQ[m][h])
                    d(ve.reciprocal(r, r))
                    d(stt(H[:, y0 + h, :], PS[bank + h][:], gain, r, ALU.mult, ALU.mult))
                    d(ve.tensor_tensor(H[:, y0 + h, :], H[:, y0 + h, :], tile(gate0 + h), ALU.mult), "yh", m, h)

            def invert(m):
                lt, xs, xts, nts, _ = INV[m[0]]
                n, b = LEVELS * len(lt), len(lt)
                ident = mask4("ident")
                for h in range(b):
                    d(ve.tensor_copy(by_tt(xs[h]), ident), chain=False)
                    d(ve.tensor_copy(by_tt(xts[h]), ident))

                def update(q):
                    h, bank = q % b, 3 * (q % 2)
                    dve.wait_ge(*pe_done("xnx", m, q))
                    if q < n - b:
                        d(ve.tensor_tensor(xs[h], xs[h], PS[bank + 1][:], ALU.subtract), chain=False)
                    d(ve.tensor_tensor(xts[h], xts[h], PS[bank + 2][:], ALU.subtract))

                for q in range(n):
                    d(ve.tensor_tensor(by_tt(nts[q % 2]), by_tt(lt[q % b]), mask4(f"lev{q // b}"), ALU.mult), "nT", m, q)
                    if q:
                        update(q - 1)
                update(n - 1)
                d(ve.memset(STAT[:, 3, 0:1], 0.0), "inv", m)

            def linear_attention():
                dve.wait_ge(tile_copied, COPIED["mix0"] + N_EVEN)
                for j in range(2):
                    dve.wait_ge(*act_done("lsig", j))
                    d(stt(tile(29 + j), tile(29 + j), 0.0, tile(31 + j), ALU.min, ALU.subtract))
                    d(ve.tensor_tensor_scan(tile(31 + j), cst("reset"), tile(29 + j), 0.0, ALU.mult, ALU.add))
                    b = by_chunk(tile(31 + j))
                    d(ve.tensor_tensor(by_chunk(tile(33 + j)), b[:, :, CH - 1:CH].broadcast_to([P, NCH, CH]), b,
                                       ALU.subtract), "dl", j)
                for j in range(2):
                    dve.wait_ge(*act_done("gexp", j))
                    d(stt(tile(GQ0 + j), tile(GQ0 + j), 0.125, tile(35 + j), ALU.mult, ALU.mult))
                    d(ve.tensor_tensor(tile(33 + j), tile(33 + j), tile(GK0 + j), ALU.mult), "kdec", j)
                    d(ve.tensor_tensor(tile(GK0 + j), tile(GK0 + j), tile(29 + j), ALU.mult), "kn", j)
                for j in range(2):
                    dve.wait_ge(*pe_done("kv", j))
                    for c in range(NCH - 1):
                        kv = PS[4 + 2 * j + c // 4][:, col(c % 4)]
                        last = ("states",) if j == 1 and c == NCH - 2 else ()
                        if c == 0:
                            d(ve.tensor_copy(gla_state(j, 1), kv))
                        else:
                            d(stt(gla_state(j, c + 1), gla_state(j, c), tile(35 + j)[:, c * CH + CH - 1:c * CH + CH], kv,
                                  ALU.mult, ALU.add), *last)
                for h in range(4):
                    dve.wait_ge(*pe_done("gatt", h))
                    dve.wait_ge(*act_done("kdT", 1))
                    d(stt(by_tt(tile(GATT[h])), by_tt(PS[h][:]), 3e38, mask4("incl"), ALU.min, ALU.mult), "gatt", h)
                dve.wait_ge(*act_done("ggate"))
                head_norms("gla", 4, 0, v("glan"), GG0)

            def delta_rule():
                for t in range(12):
                    x, y = tile(DQ0 + t), tile(t)
                    d(ve.tensor_scalar(y, x, v("gdnconv", 36 + t), None, ALU.mult))
                    for lag in range(1, 4):
                        d(stt(y[:, lag:T], x[:, 0:T - lag], v("gdnconv", 12 * (3 - lag) + t), y[:, lag:T], ALU.mult, ALU.add),
                          *(("dconv", t) if lag == 3 else ()))
                d(ve.memset(tile(22), 0.0), "rows0")
                g, e = slice(DA_ROW, DA_ROW + 4), slice(ED_ROW, ED_ROW + 4)
                dve.wait_ge(*act_done("dsp"))
                d(stt(tile(SM0)[g], tile(SM0)[g], 0.0, tile(21)[g], ALU.max, ALU.add))
                d(ve.tensor_scalar(tile(SM0)[g], tile(SM0)[g], STAT[g, 0, 0:1], -1.0, ALU.mult, ALU.mult))
                d(ve.tensor_tensor_scan(tile(22)[g], cst("reset")[g], tile(SM0)[g], 0.0, ALU.mult, ALU.add))
                b = by_chunk(tile(22))[g]
                dve.wait_ge(*act_done("beta"))
                d(ve.tensor_tensor(by_chunk(tile(22))[e], b[:, :, CH - 1:CH].broadcast_to([4, NCH, CH]), b,
                                   ALU.subtract), "gc")
                for t in range(8):
                    dve.wait_ge(*act_done("l2sd", t))
                    d(ve.reciprocal(tile(13 + t), tile(13 + t)))
                    d(stt(tile(t), tile(t), 128 ** -0.5 if t < 4 else 1.0, tile(13 + t), ALU.mult, ALU.mult), "l2n", t)
                dve.wait_ge(*act_done("cols"))
                for tt in range(TT):
                    cols = tile(23)[:, col(tt)]
                    d(ve.tensor_tensor(STAT[:, 1, 4 * tt:4 * tt + 4], cols[:, EG_ROW:EG_ROW + 4],
                                       cols[:, DB_ROW:DB_ROW + 4], ALU.mult), *(("colbe",) if tt == TT - 1 else ()))
                for h in range(4):
                    dve.wait_ge(*act_done("egb", h))
                    for tt in range(TT):
                        c = tt * P + DA_ROW + h
                        d(ve.tensor_scalar(tile(29 + h)[:, col(tt)], PS[h][:, col(tt)], tile(23)[:, c:c + 1], 0.0,
                                           ALU.subtract, ALU.min), *(("ddec", h) if tt == TT - 1 else ()), chain=False)
                for h in range(4):
                    d(ve.tensor_tensor(tile(37 + h), tile(4 + h), PS[4 + h][:], ALU.mult), "kb", h)
                    dve.wait_ge(*act_done("ddec", h))
                    d(ve.tensor_tensor(by_tt(tile(29 + h)), by_tt(tile(29 + h)), mask4("incl"), ALU.mult))
                    d(ve.tensor_tensor(tile(13 + h), tile(h), tile(33 + h), ALU.mult))
                for h in range(4):
                    dve.wait_ge(*pe_done("datt", h))
                    d(ve.tensor_tensor(tile(h), PS[h][:], tile(29 + h), ALU.mult))
                    d(ve.tensor_tensor(tile(17 + h), PS[4 + h][:], tile(29 + h), ALU.mult))
                    d(ve.tensor_tensor(by_tt(tile(17 + h)), by_tt(tile(17 + h)), mask4("strict"), ALU.mult), "dLT", h)
                dve.wait_ge(*pe_done("dtok", 3))
                dve.wait_ge(*act_done("dtok", 3))
                invert(("gdn", 0))
                dve.wait_ge(*act_done("du", 3))
                for c in range(NCH):
                    r, tt = slice(CH * (c % 2), CH * (c % 2) + CH), c // 2
                    if c == 0:
                        d(ve.tensor_copy(tile(8)[r], tile(17)[r]), "dv", c)
                    else:
                        dve.wait_ge(*pe_done("dws", c))
                        d(ve.tensor_tensor(tile(8 + tt)[r], tile(17 + tt)[r], PS[0][r, :], ALU.subtract), "dv", c)
                    if c < NCH - 1:
                        dve.wait_ge(*pe_done("dupd", c))
                        if c == 0:
                            d(ve.tensor_copy(STATE[:], PS[1][:]), "dstate", c)
                        else:
                            for h in range(4):
                                d(stt(STATE[:, col(h)], STATE[:, col(h)], tile(33 + h)[:, c * CH + CH - 1:c * CH + CH],
                                      PS[1][:, col(h)], ALU.mult, ALU.add), *(("dstate", c) if h == 3 else ()),
                                  chain=(h == 3))
                head_norms("gdn", 4, 4, v("gdnn"), DZ0)

            def lru():
                dve.wait_ge(tile_copied, COPIED["mix1"] + N_ODD)
                for j in range(4):
                    x, y = tile(LX0 + j), tile(22 + j)
                    d(ve.tensor_scalar(y, x, v("lconv", 12 + j), v("lconvb", j), ALU.mult, ALU.add))
                    for lag in range(1, 4):
                        d(stt(y[:, lag:T], x[:, 0:T - lag], v("lconv", 4 * (3 - lag) + j), y[:, lag:T], ALU.mult, ALU.add),
                          *(("lconv", j) if lag == 3 else ()))
                dve.wait_ge(*act_done("lam"))
                z, s, s2, acc = (LRUV[:, 4 * i:4 * i + 4] for i in range(4))
                d(ve.tensor_scalar(s, z, 2.0, None, ALU.add))
                d(ve.reciprocal(s, s))
                d(ve.tensor_tensor(s, s, z, ALU.mult))
                d(ve.tensor_tensor(s2, s, s, ALU.mult))
                d(ve.tensor_scalar(acc, s2, 1 / 17, 1 / 15, ALU.mult, ALU.add))
                for n in (13, 11, 9, 7, 5, 3, 1):
                    d(ve.tensor_tensor(acc, acc, s2, ALU.mult))
                    d(ve.tensor_scalar(acc, acc, 1 / n, None, ALU.add))
                d(ve.tensor_tensor(acc, acc, s, ALU.mult))
                d(ve.tensor_scalar(z, v4("lam"), -1.0, 0.0, ALU.mult, ALU.max))
                d(stt(z, acc, 2.0, z, ALU.mult, ALU.add))
                d(ve.tensor_scalar(LRUV[:, 8:12], z, -8.0, None, ALU.mult))
                d(ve.tensor_scalar(LRUV[:, 12:16], z, 8.0, None, ALU.mult), "lam")
                for j in range(4):
                    g, y = tile(14 + j), tile(LY0 + j)
                    d(ve.tensor_tensor(g, y, y, ALU.mult))
                    d(ve.tensor_scalar(g, g, 0.044715, 1.0, ALU.mult, ALU.add))
                    d(ve.tensor_tensor(g, g, y, ALU.mult), "gelu0", j)
                for j in range(4):
                    dve.wait_ge(*act_done("ltanh", j))
                    m = tile(38 + j)
                    d(ve.tensor_scalar(m, tile(26 + j), 1.0, None, ALU.add))
                    d(ve.reciprocal(m, m))
                    d(stt(m, tile(26 + j), 2.0, m, ALU.mult, ALU.mult))
                    d(ve.tensor_scalar(m, m, 0.0, None, ALU.max), "lmult", j)
                for j in range(4):
                    dve.wait_ge(*act_done("gelu", j))
                    d(stt(tile(14 + j), tile(14 + j), 1.0, tile(LY0 + j), ALU.add, ALU.mult))
                    dve.wait_ge(*act_done("lmult", j))
                    d(ve.tensor_tensor(tile(38 + j), tile(38 + j), tile(30 + j), ALU.mult))
                    d(ve.tensor_tensor(tile(38 + j), tile(38 + j), tile(22 + j), ALU.mult))
                    d(ve.tensor_tensor_scan(tile(30 + j), tile(34 + j), tile(38 + j), 0.0, ALU.mult, ALU.add))
                    d(stt(H[:, 4 + j, :], tile(30 + j), 0.5, tile(14 + j), ALU.mult, ALU.mult))

            def rwkv():
                n = LX0
                d(ve.tensor_tensor(BIG[:, 22:22 + n, 1:T], BIG[:, 0:n, 0:T - 1], BIG[:, 0:n, 1:T], ALU.subtract),
                  chain=False)
                d(ve.tensor_scalar(BIG[:, 22:22 + n, 0:1], BIG[:, 0:n, 0:1], -1.0, None, ALU.mult))
                for t in (WA0, GL0, *range(WA0)):
                    d(stt(tile(t), tile(22 + t), v("mu", t), tile(t), ALU.mult, ALU.add), "shift", t)
                for j in range(4):
                    d(ve.tensor_scalar(tile(36 + j), tile(RK0 + j), v("kk", j), None, ALU.mult), "kk", j)
                for j in range(4):
                    dve.wait_ge(*act_done("rgate", j))
                    dve.wait_ge(*act_done("kksd", j))
                    d(ve.reciprocal(tile(40 + j), tile(40 + j)))
                    d(ve.tensor_tensor(tile(36 + j), tile(36 + j), tile(40 + j), ALU.mult))
                    d(ve.tensor_scalar(tile(40 + j), tile(28 + j), 1.0, v("ka", j), ALU.subtract, ALU.mult))
                    d(stt(tile(RK0 + j), tile(40 + j), 1.0, tile(RK0 + j), ALU.add, ALU.mult))
                    d(stt(tile(14 + j), tile(R0 + j), v("rk", j), tile(RK0 + j), ALU.mult, ALU.mult), "bonus0", j)
                for j in range(4):
                    dve.wait_ge(*pe_done("bonus", j))
                    d(ve.tensor_tensor(tile(14 + j), PS[4 + j][:], tile(RV0 + j), ALU.mult))
                for j in range(4):
                    d(ve.tensor_tensor_scan(tile(40 + j), cst("reset"), tile(24 + j), 0.0, ALU.mult, ALU.add))
                    b = by_chunk(tile(40 + j))
                    d(ve.tensor_tensor(tile(24 + j), tile(40 + j), tile(24 + j), ALU.subtract))
                    d(ve.tensor_tensor(by_chunk(tile(18 + j)), b[:, :, CH - 1:CH].broadcast_to([P, NCH, CH]), b,
                                       ALU.subtract))
                    d(ve.tensor_tensor(tile(28 + j), tile(28 + j), tile(36 + j), ALU.mult), "rcum", j)
                for j in range(4):
                    dve.wait_ge(*act_done("rexp", j))
                    d(stt(tile(24 + j), tile(36 + j), -1.0, tile(24 + j), ALU.mult, ALU.mult))
                    d(ve.tensor_tensor(tile(j), tile(j), tile(32 + j), ALU.mult))
                    d(ve.tensor_copy(STAT[:, 2, 8 * j:8 * j + 8], by_chunk(tile(32 + j))[:, :, CH - 1]))
                    d(ve.tensor_tensor(tile(36 + j), tile(28 + j), tile(40 + j), ALU.mult))
                    d(ve.tensor_tensor(tile(28 + j), tile(28 + j), tile(18 + j), ALU.mult))
                    d(ve.tensor_tensor(tile(18 + j), tile(18 + j), tile(4 + j), ALU.mult))
                    d(ve.tensor_tensor(tile(4 + j), tile(4 + j), tile(40 + j), ALU.mult),
                      *(("rprep",) if j == 3 else ()))
                for tt in range(TT):
                    m = ("rwkv", tt)
                    dve.wait_ge(*pe_done("rmat", tt))
                    for g in range(2):
                        d(stt(by_tt(INV["rwkv"][0][g]), by_tt(PS[4 + g][:]), -1.0, mask4("strict"), ALU.mult, ALU.mult),
                          chain=False)
                        d(ve.tensor_tensor(by_tt(RT["aak"][g]), by_tt(PS[6 + g][:]), mask4("strict"), ALU.mult),
                          *(("rmat", tt) if g else ()))
                    dve.wait_ge(*pe_done("rz", tt))
                    invert(m)
                    dve.wait_ge(*pe_done("rout", tt))
                    for g in range(2):
                        d(ve.tensor_tensor(by_tt(RT["rb"][g]), by_tt(PS[4 + g][:]), mask4("incl"), ALU.mult), chain=False)
                        d(ve.tensor_tensor(by_tt(RT["rk"][g]), by_tt(PS[6 + g][:]), mask4("incl"), ALU.mult),
                          *(("rout", tt) if g else ()))
                    dve.wait_ge(*act_done("ru", tt))
                    for c in (2 * tt, 2 * tt + 1):
                        r = slice(CH * (c % 2), CH * (c % 2) + CH)
                        if c:
                            dve.wait_ge(*pe_done("rws", c))
                            d(ve.tensor_tensor(RT["z"][r], RT["z"][r], PS[3][r, :], ALU.add), "ruc", c)
                        else:
                            d(ve.memset(STAT[:, 3, 0:1], 0.0), "ruc", c)
                        if c < NCH - 1:
                            dve.wait_ge(*pe_done("rupd", c))
                            if c == 0:
                                d(ve.tensor_copy(STATE[:, 0:256], PS[1][:, 0:256]), "rstate", c)
                            else:
                                for j in range(4):
                                    d(stt(STATE[:, col(j, 64)], STATE[:, col(j, 64)],
                                          STAT[:, 2, 8 * j + c:8 * j + c + 1], PS[1][:, col(j, 64)],
                                          ALU.mult, ALU.add), *(("rstate", c) if j == 3 else ()), chain=(j == 3))
                for j in range(4):
                    dve.wait_ge(*pe_done("gmean", j))
                    dve.wait_ge(*act_done("ry", TT - 1))
                    d(ve.tensor_tensor(tile(j), tile(j), PS[j][:], ALU.subtract), "gcentred", j, chain=False)
                for j in range(4):
                    dve.wait_ge(*act_done("gsd", j))
                    d(ve.reciprocal(tile(22 + j), tile(22 + j)))
                    d(stt(tile(j), tile(j), v("lnw", j), tile(22 + j), ALU.mult, ALU.mult))
                    d(stt(tile(j), tile(j), v("lnbb", j), tile(14 + j), ALU.add, ALU.add))
                    dve.wait_ge(*pe_done("gout", j))
                    d(ve.tensor_tensor(H[:, j, :], tile(j), PS[j][:], ALU.mult))

            modulation()
            for l in range(DEPTH):
                layer_norm(("ln", l), l, True)
                rope_and_attention(l)
                short_conv(l)
                for j in range(2):
                    dve.wait_ge(*pe_done("four", l, j))
                    d(ve.tensor_tensor(H[:, 6 + j, :], PS[4 + j][:], tile(GF0 + j), ALU.mult),
                      *(("y", "first", l) if j else ()))
                residual(l)
                layer_norm(("pln", l), l, False)
            for i in range(DEPTH):
                pre_norm(f"{i}0", 6 * i)
                ffn(f"{i}0")
                post_norm(f"{i}0", 6 * i + 1, lambda k: H[:, k, :], 0.5)
                pre_norm(f"mix{i}", 6 * i + 2)
                if i % 2 == 0:
                    linear_attention()
                    delta_rule()
                else:
                    lru()
                    rwkv()
                d(ve.memset(STAT[:, 3, 0:1], 0.0), "y", "mix", i)
                dve.wait_ge(tile_copied, COPIED[f"mixout{i}"] + KT)
                post_norm(f"mix{i}", 6 * i + 3, tile, 1.0)
                pre_norm(f"{i}1", 6 * i + 4)
                ffn(f"{i}1")
                post_norm(f"{i}1", 6 * i + 5, lambda k: H[:, k, :], 0.5)
            d(ve.memset(STAT[:, 3, 0:1], 0.0), "x", "end")

    return seen


def _units(w, k_tiles=KT):
    k, n = w.shape
    return w.reshape(k_tiles, P, n // P, P).transpose(2, 1, 0, 3).reshape(n // P, P, k_tiles * P)


def _columns(a):
    return a.reshape(-1, P).T


def _heads_order():
    return np.concatenate([np.arange(h * 64, h * 64 + 64) for t in range(4) for h in (t, 4 + t)])


def _weights(a):
    heads, k_units, d_units = _heads_order(), [], []
    for l in range(DEPTH):
        k_units.append(_units(a["w_ada"][l]))
    for l in range(DEPTH):
        w = a["w_in"][l]
        k_units.append(_units(np.concatenate([w[:, heads], w[:, 512:768], w[:, 768 + heads], w[:, 1280:]], 1)))
        w = a["w_out"][l]
        k_units.append(_units(np.concatenate([w[heads], w[512:]], 0)))

    def ffn(i, j):
        g, u = _units(a["ffn_w_gate_2"][i, j]), _units(a["ffn_w_up_2"][i, j])
        k_units.append(np.stack([g, u], 1).reshape(2 * FT, P, UNIT))
        w = a["ffn_w_down_2"][i, j].reshape(2, KD, P, KT, P)
        d_units.append(w.transpose(3, 0, 2, 1, 4).reshape(2 * KT, P, UNIT_D))

    for i in range(DEPTH):
        ffn(i, 0)
        if i % 2 == 0:
            w = a["even_w_in_2"][i // 2]
            small = np.zeros((D, P), w.dtype)
            small[:, GLR_ROW:GLR_ROW + 16] = w[:, 1536:1552]
            small[:, DA_ROW:DA_ROW + 4] = w[:, 3600:3604]
            small[:, DB_ROW:DB_ROW + 4] = w[:, 3604:3608]
            k_units.append(_units(np.concatenate([w[:, :1536], small, w[:, 1552:3600]], 1)))
            k_units.append(_units(a["even_w_out_2"][i // 2]))
        else:
            k_units.append(_units(a["odd_w_in_2"][i // 2]))
            k_units.append(_units(a["odd_w_out_2"][i // 2]))
        ffn(i, 1)
    return np.concatenate(k_units), np.concatenate(d_units)


def _vectors(a):
    dt = a["x"].dtype
    out = np.zeros((P, NV), dt)

    def put(name, x, rows=slice(None)):
        out[rows, VCOL[name]:VCOL[name] + x.shape[1]] = x

    put("c", _columns(a["c"][0]))
    put("bada", np.concatenate([_columns(b) for b in a["b_ada"]], 1))
    put("qg", np.concatenate([a["q_gain"], a["q_gain"]], 1).T)
    put("kg", np.concatenate([a["k_gain"], a["k_gain"]], 1).T)
    put("cw", np.concatenate([_columns(w) for w in a["conv_w"]], 1))
    put("lng", np.concatenate([_columns(w) for w in a["ln_g"]], 1))
    put("lnb", np.concatenate([_columns(w) for w in a["ln_b"]], 1))
    put("nw", _columns(a["norm_w_2"]))
    put("lorab", _columns(a["gla_lora_b_2"]))
    put("glan", _columns(a["gla_norm_2"]))
    put("gdnconv", _columns(a["gdn_conv_2"]))
    put("alog", a["gdn_a_log_2"].T, slice(DA_ROW, DA_ROW + 4))
    put("dtb", a["gdn_dt_bias_2"].T, slice(DA_ROW, DA_ROW + 4))
    put("gdnn", _columns(a["gdn_norm_2"]))
    for name, key in (("mu", "rwkv_mu"), ("w0", "rwkv_w0"), ("a0", "rwkv_a0"), ("kk", "rwkv_k_k"), ("ka", "rwkv_k_a"),
                      ("rk", "rwkv_r_k"), ("lnw", "rwkv_ln_w"), ("lnbb", "rwkv_ln_b"), ("lconv", "lru_conv_w"),
                      ("lconvb", "lru_conv_b"), ("lba", "lru_ba"), ("lbx", "lru_bx"), ("lam", "lru_lambda")):
        put(name, _columns(a[key + "_2"]))
    for name, value in (("eps6", 1e-6), ("eps5", 1e-5), ("epsg", 64e-5), ("one", 1.0)):
        out[:, VCOL[name]] = value
    return out


def _small_weights(a):
    dt = a["x"].dtype
    out = np.zeros((P, NS), dt)
    for l in range(DEPTH):
        for g in range(4):
            j, s = g // 2, 64 * (g % 2)
            c = SCOL["fmix"] + l * 2 * P + j * P + s
            out[s:s + 64, c:c + 64] = a["f_mix"][l, g]
    out[0:16, SCOL["lora"]:SCOL["lora"] + 2 * P] = a["gla_lora_w2_2"][0]
    out[0:64, SCOL["wa2"]:SCOL["wa2"] + 4 * P] = a["rwkv_w2_2"][0]
    out[64:128, SCOL["wa2"]:SCOL["wa2"] + 4 * P] = a["rwkv_a2_2"][0]
    out[:, SCOL["g2"]:SCOL["g2"] + 4 * P] = a["rwkv_g2_2"][0]
    for b in range(8):
        j, s = b // 2, 64 * (b % 2)
        for name, key in (("lwa", "lru_wa_2"), ("lwx", "lru_wx_2")):
            c = SCOL[name] + j * P + s
            out[s:s + 64, c:c + 64] = a[key][0, b]
    return out


def _constants():
    f32 = np.float32
    out = np.zeros((P, NC), f32)

    def put(name, x):
        c, n = CCOL[name]
        out[:, c:c + n] = x

    half = 32
    inv_freq = (f32(1.0) / (f32(10000.0) ** (np.arange(0, half, 2, dtype=f32) / f32(half)))).astype(f32)
    row, column = np.arange(T) // 64, np.arange(T) % 64
    p = np.arange(P)
    position = np.where((p % 64 < half)[:, None], row, column).astype(f32)
    angle = position * inv_freq[p % 16][:, None]
    put("cos", np.cos(angle))
    put("sin", np.sin(angle))
    perm = np.zeros((P, P), f32)
    first = p % 32 < 16
    perm[p[first] + 16, p[first]] = -1.0
    perm[p[~first] - 16, p[~first]] = 1.0
    put("perm", perm)
    put("reset", (np.arange(T) % CH != 0).astype(f32))
    key, query = p[:, None], p[None, :]
    same = key // CH == query // CH
    put("ident", np.eye(P))
    put("incl", same & (query >= key))
    put("strict", same & (query > key))
    for b in range(LEVELS):
        w = 1 << b
        put(f"lev{b}", (key // (2 * w) == query // (2 * w)) & (key // w % 2 == 0) & (query // w % 2 == 1))
    put("onesD", 1.0 / D)
    put("ones128", 1.0 / P)
    put("ones1", 1.0)
    put("blk1", (key // 64 == query // 64))
    put("blk64", (key // 64 == query // 64) / 64.0)
    for h in range(4):
        c = CCOL["sel"][0] + h * P
        out[DA_ROW + h, c:c + P] = 1.0
        out[DB_ROW + h, c:c + P] = 1.0
    d = np.arange(64)
    turn = 2 * np.pi * ((d[:, None] * d[None, :]) % 64) / 64
    for name, m in (("c64", np.cos(turn)), ("s64", np.sin(turn))):
        put(name, np.kron(np.eye(2), m))
    t = np.arange(T)
    turn = 2 * np.pi * ((t[:, None] * t[None, :]) % T) / T
    scale = 1.0 / np.sqrt(T * 64.0)
    dft = np.stack([np.cos(turn) * scale, -np.sin(turn) * scale])
    dft = dft.reshape(2, TT, P, T).transpose(2, 0, 1, 3).reshape(P, 2 * TT, T)
    return out, dft.astype(f32)


def kernel(**inputs):
    import numpy as _np
    import concourse.bacc as _bacc
    from concourse import mybir as _mybir
    from concourse.bass_utils import run_bass_kernel_spmd as _run

    a = {name: _np.asarray(x) for name, x in inputs.items()}
    w_k, w_d = _weights(a)
    constants, dft = _constants()
    x = a["x"][0].T.reshape(KT, P, T).transpose(1, 0, 2)
    arrays = {"x_in": x, "w_k": w_k, "w_d": w_d, "vec_in": _vectors(a), "cst_in": constants,
              "small_in": _small_weights(a), "dft_in": dft}
    arrays = {name: _np.ascontiguousarray(v) for name, v in arrays.items()}

    def program(known):
        nc = _bacc.Bacc("TRN2", target_bir_lowering=False, num_devices=1)
        args = [nc.dram_tensor(name, v.shape, _mybir.dt.from_np(v.dtype), kind="ExternalInput").ap()
                for name, v in arrays.items()]
        out = nc.dram_tensor("out_0_dram", (P, KT, T), _mybir.dt.from_np(_np.dtype("float32")),
                             kind="ExternalOutput").ap()
        return nc, write_program(nc, known, *args, out)

    _, known = program({})
    nc, _ = program(known)
    r = _run(nc, [arrays], core_ids=[0])
    y = r.results[0]["out_0_dram"]
    return y.transpose(1, 0, 2).reshape(D, T).T.reshape(1, T, D)
```

```python
from contextlib import ExitStack

import numpy as np

import concourse.bass as bass
from concourse import mybir

F32 = mybir.dt.float32
F32R = mybir.dt.float32r
ALU = mybir.AluOpType
ACT = mybir.ActivationFunctionType
AX_X = mybir.AxisListType.X

P = 128
D = 1024
T = 512
KT = D // P
TT = T // P
DEPTH = 2
ALPHA = (2 * DEPTH) ** 0.25
CH = 64
NCH = T // CH
D_FF = 2816
FT = D_FF // P
HALVES = (12, 10)
SLOTS = 4
SPLIT = 2
UNIT = KT * P
LEVELS = 6
DECAY = float(np.exp(-0.5))

Q0, K0, V0, GA0, CU0, CB0, CC0, GC0, FU0, GF0, N_FIRST = 0, 4, 5, 6, 10, 12, 14, 16, 18, 20, 22
GQ0, GK0, GV0, GG0, SM0, DQ0, DK0, DV0, DZ0, N_EVEN = 0, 2, 4, 8, 12, 13, 17, 21, 25, 29
GLR_ROW, DA_ROW, DB_ROW, EG_ROW, ED_ROW = 0, 32, 64, 0, 96
R0, RK0, RV0, WA0, GL0, LX0, LY0, N_ODD = 0, 4, 8, 12, 13, 14, 18, 22

STREAM = []
for _l in range(DEPTH):
    STREAM += [(f"first{_l}", N_FIRST, "k"), (f"firstout{_l}", KT, "k")]
for _i in range(DEPTH):
    for _j in range(2):
        for _q, _half in enumerate(HALVES):
            STREAM += [(f"ffn{_i}{_j}{_q}", 2 * _half, "k"), (f"down{_i}{_j}{_q}", 2 * KT, f"d{_q}")]
        if _j == 0:
            STREAM += [(f"mix{_i}", (N_EVEN, N_ODD)[_i % 2], "k"), (f"mixout{_i}", KT, "k")]
STREAM.append(("end", SPLIT, "k"))
UNIT0, _n = {}, 0
for _name, _count, _kind in STREAM:
    UNIT0[_name] = _n
    _n += _count
N_UNITS = _n - SPLIT
IN_ARRAY, _m = {}, {"k": 0, "d0": 0, "d1": 0}
for _name, _count, _kind in STREAM:
    IN_ARRAY[_name] = _m[_kind]
    _m[_kind] += _count
WIDTH = {"k": UNIT, "d0": HALVES[0] // 2 * P, "d1": HALVES[1] // 2 * P}

VECS = [("c", 8), ("bada", 48), ("qg", 2), ("kg", 2), ("cw", 12), ("lng", 16), ("lnb", 16),
        ("nw", 96), ("lorab", 2), ("glan", 1), ("gdnconv", 48), ("alog", 1), ("dtb", 1), ("gdnn", 1),
        ("mu", 14), ("w0", 4), ("a0", 4), ("kk", 4), ("ka", 4), ("rk", 4), ("lnw", 4), ("lnbb", 4),
        ("lconv", 16), ("lconvb", 4), ("lba", 4), ("lbx", 4), ("lam", 4),
        ("eps6", 1), ("eps5", 1), ("epsg", 1), ("one", 1)]
VCOL, _n = {}, 0
for _name, _count in VECS:
    VCOL[_name] = _n
    _n += _count
NV = _n

CSTS = [("cos", T), ("sin", T), ("reset", T), ("ident", P), ("incl", P), ("strict", P),
        *[(f"lev{b}", P) for b in range(LEVELS)],
        *[(f"{m}c", CH) for m in ("ident", "incl", "strict", *[f"lev{b}" for b in range(LEVELS)])], ("onesD", P), ("ones128", P), ("ones1", P),
        ("blk1", P), ("blk64", P), ("perm", P), ("sel", 4 * P), ("c64", P), ("s64", P)]
CCOL, _n = {}, 0
for _name, _count in CSTS:
    CCOL[_name] = (_n, _count)
    _n += _count
NC = _n

SMALLS = [("fmix", 2 * 2 * P), ("lora", 2 * P), ("wa2", 4 * P), ("g2", 4 * P), ("lwa", 4 * P), ("lwx", 4 * P)]
SCOL, _n = {}, 0
for _name, _count in SMALLS:
    SCOL[_name] = _n
    _n += _count
NS = _n


def step_counter(name, sem, known, seen):
    count, inside = [0], []

    def signal(step=None):
        count[0] += 1
        if step is not None:
            assert (name, step) not in seen, step
            seen[name, step] = (count[0], 0, 1)
            inside.append(step)
        return sem, 1

    def so_far():
        return sem, count[0]

    def begin_loop():
        inside[:] = []
        return count[0]

    def end_loop(first, rounds):
        body = count[0] - first
        for step in inside:
            seen[name, step] = (seen[name, step][0], body, rounds)
        count[0] = first + body * rounds

    def done(*step, i=None, lag=0):
        first, body, rounds = known.get((name, step if len(step) > 1 else step[0]), (1000, 0, 1))
        if i is None:
            return sem, first + body * (rounds - 1)
        assert not known or first - lag * body > 0, step
        return sem, i * body + (first - lag * body)

    return signal, so_far, begin_loop, end_loop, done


def write_program(nc, known, x_in, w_k, w_d0, w_d1, w_ada, vec_in, cst_in, small_in, dft_in, out):
    with ExitStack() as ctx:
        def sb(name, shape, dt=F32):
            return ctx.enter_context(nc.sbuf_tensor(name, shape, dt))

        def sem(name):
            return ctx.enter_context(nc.semaphore(name))

        X = sb("residual", [P, KT, T])
        with nc.sbuf_tensor("work", [P, 48, T], F32) as BIG:
            pass
        HID = sb("hidden", [P, 24, T], F32R)
        sb("outputs", [P, 8, T])
        H = sb("normed", [P, 2 * KT, T], F32R)
        RING = sb("ring", [P, SLOTS, UNIT])
        WH = sb("weights_high", [P, SPLIT, UNIT], F32R)
        WL = sb("weights_low", [P, SPLIT, UNIT], F32R)
        CST = sb("constants", [P, NC])
        VEC = sb("vectors", [P, NV])
        SMALL = sb("small_weights", [P, NS])
        GATE = sb("silu_gate", [P, 4, T])
        RSTD = sb("rstd", [P, 2, T])
        MOD = sb("modulation", [P, 2, 24])
        STAT = sb("softmax_stats", [P, 4, 32])
        LRUV = sb("lru_vectors", [P, 16])
        STATE = sb("state", [P, 4 * P])
        PS = [ctx.enter_context(nc.psum_tensor(f"bank{i}", [P, T], F32)) for i in range(8)]

        w_loaded = [sem(f"w_loaded{i}") for i in range(SLOTS)]
        unit_high = sem("unit_high")
        unit_split = sem("unit_split")
        unit_used = sem("unit_used")
        ada_in = [sem(f"ada_in{i}") for i in range(3)]
        tile_copied = sem("tile_copied")
        consts_in = sem("consts_in")
        dft_in_s = sem("dft_in")
        out_stored = sem("out_stored")
        seen = {}
        pe_signal, pe_so_far, pe_begin_loop, pe_end_loop, pe_done = step_counter("pe", sem("pe_steps"), known, seen)
        act_signal, act_so_far, act_begin_loop, act_end_loop, act_done = step_counter("act", sem("act_steps"), known, seen)
        dve_signal, dve_so_far, dve_begin_loop, dve_end_loop, dve_done = step_counter("dve", sem("dve_steps"), known, seen)

        def v(name, j=0):
            return VEC[:, VCOL[name] + j:VCOL[name] + j + 1]

        def cst(name, a=0, b=None):
            c, n = CCOL[name]
            return CST[:, c + a:c + (n if b is None else b)]

        def tile(i):
            return BIG[:, i, :]

        def by_tt(ap):
            return ap.rearrange("p (t c) -> p t c", t=TT)

        def by_chunk(ap):
            return ap.rearrange("p (n c) -> p n c", c=CH)

        def mask4(name):
            return cst(name).unsqueeze(1).broadcast_to([P, TT, P])

        def mask_chunks(name):
            return cst(name + "c").unsqueeze(1).broadcast_to([P, 4, CH])

        def col(tt, w=P):
            return slice(tt * w, tt * w + w)

        def loaded(u, i=None):
            value = 16 * (u // SLOTS + 1)
            return w_loaded[u % SLOTS], value if i is None else i * 16 + value

        def units(sem, u, i=None):
            return sem, u + 1 if i is None else i * SLOTS + (u + 1)

        COPIED, n_copied = {}, 0
        for name, count, _ in STREAM:
            if name.startswith(("first", "mix")):
                COPIED[name] = n_copied
                n_copied += count

        def token_major(name):
            if name in ("first0", "first1"):
                return V0, V0 + 1
            if name == "mix0":
                return GV0, GV0 + 4
            return 0, 0

        def segments(name):
            count = dict((n, c) for n, c, _ in STREAM)[name]
            first, end_tm = token_major(name)
            runs, at = [], 0
            for end, is_tm in ((first, False), (end_tm, True), (count, False)):
                if (end - at) // SLOTS > 1:
                    g = (end - at) // SLOTS
                    runs.append((at, g, SLOTS, is_tm))
                    at += g * SLOTS
                if end > at:
                    runs.append((at, 1, end - at, is_tm))
                    at = end
            return runs

        def v4(name):
            return VEC[:, VCOL[name]:VCOL[name] + 4]

        Y_FIRST = [0, 1, 2, 3, 10, 11, 18, 19]
        Y_MIX = [[44, 45, 46, 47, 25, 26, 27, 28], [44, 45, 46, 47, 0, 1, 2, 3]]
        GATT = [29, 30, 33, 34]
        HSQ = {"gla": [35, 36, 41, 42], "gdn": [0, 1, 2, 3]}

        def gla_state(j, c):
            return tile(37 + 2 * j + (c - 1) // 4)[:, col((c - 1) % 4)]

        INV = {"gdn": ([tile(i) for i in (17, 18, 19, 20)], [tile(i) for i in (41, 42, 43, 24)],
                       [tile(i) for i in (4, 5, 6, 7)], [tile(21), tile(12)], [tile(22), tile(23)]),
               "rwkv": tuple([tile(i)[:, 0:256], tile(i)[:, 256:512]] for i in (33, 34, 35, 40, 41))}
        RT = {"a": tile(22), "v": tile(23), "bd": tile(12), "kd": tile(32), "z": tile(43), "w": tile(40),
              "aak": tile(42), "rb": tile(33), "rk": tile(34)}

        def hc(h):
            return slice((h % 2) * 256 + h // 2 * 64, (h % 2) * 256 + h // 2 * 64 + 64)

        block = ctx.enter_context(nc.Block())

        @block.sync
        def _(sp):
            sp.dma_start(CST[:], cst_in).then_inc(consts_in, 16)
            sp.dma_start(VEC[:], vec_in).then_inc(consts_in, 16)
            sp.dma_start(X[:], x_in).then_inc(consts_in, 16)
            sp.dma_start(SMALL[:], small_in).then_inc(consts_in, 16)

            for q in range(6):
                if q >= 3:
                    sp.wait_ge(*pe_done("modrow", q - 3))
                sp.dma_start(BIG[:, 16 * (q % 3):16 * (q % 3) + 16, :], w_ada[q]).then_inc(ada_in[q % 3], 16)

            views = {"k": w_k.rearrange("u p n -> p u n"), "d0": w_d0.rearrange("u p n -> p u n"),
                     "d1": w_d1.rearrange("u p n -> p u n")}

            def load(name, kind, j, i=None):
                u = UNIT0[name] + j
                at = IN_ARRAY[name] + j
                if u >= SLOTS:
                    sp.wait_ge(*units(unit_split, u - SLOTS, i))
                where = at if i is None else i * SLOTS + at
                sp.dma_start(RING[:, u % SLOTS:u % SLOTS + 1, 0:WIDTH[kind]],
                             views[kind][:, bass.ds(where, 1), :]).then_inc(w_loaded[u % SLOTS], 16)

            for name, count, kind in STREAM:
                peeled = SLOTS if name == "first0" else 0
                for j in range(peeled):
                    load(name, kind, j)
                groups = (count - peeled) // SLOTS
                if groups:
                    with sp.Fori(0, groups, 1) as i:
                        for j in range(SLOTS):
                            load(name, kind, peeled + j, i)
                for j in range(peeled + groups * SLOTS, count):
                    load(name, kind, j)
            sp.wait_ge(*dve_done("x", "end"))
            sp.dma_start(out, X[:]).then_inc(out_stored, 16)
            sp.wait_ge(out_stored, 16)

        @block.gpsimd
        def _(pool):
            for l in range(DEPTH):
                pool.wait_ge(tile_copied, COPIED[f"first{l}"] + N_FIRST)
                pool.dma_start(BIG[:, 34:42, :], dft_in).then_inc(dft_in_s, 16)

        @block.tensor
        def _(pe):
            def mm(o, lhsT, rhs, start=True, stop=True):
                return pe.matmul(o, lhsT, rhs, start=start, stop=stop, skip_group_check=True)

            def step(ins, *name):
                ins.then_inc(*pe_signal(name if len(name) > 1 else name[0]))

            def drain(ins):
                ins.then_inc(*pe_signal())
                pe.wait_ge(*pe_so_far())

            def modulation(q):
                pe.wait_ge(ada_in[q % 3], 16 * (q // 3 + 1))
                if q >= 3:
                    pe.wait_ge(*dve_done("modrow", q - 3))
                for side in range(2):
                    for k in range(KT):
                        ins = mm(PS[2 * (q % 3) + side][0:1, :], v("c", k), tile(16 * (q % 3) + 2 * k + side),
                                 start=(k == 0), stop=(k == KT - 1))
                step(ins, "modrow", q)

            def modulation_columns(q):
                pe.wait_ge(*dve_done("modrow", q))
                for u in range(8):
                    row = GATE[0:1, 2 * (q % 2) + u // 4, col(u % 4)]
                    ins = mm(PS[7][:, 8 * q + u:8 * q + u + 1], row, v("one")[0:1])
                step(ins, "mod", q)

            def product(o, wh, wl, h, low, start, stop):
                mm(o, wh, h, start=start, stop=False)
                mm(o, wh, low, start=False, stop=False)
                return mm(o, wl, h, start=False, stop=stop)

            def project(name):
                def unit(j, i, is_tm):
                    u, c = UNIT0[name] + j, COPIED[name] + j
                    pe.wait_ge(*units(unit_split, u, i))
                    if c >= 4:
                        pe.wait_ge(tile_copied, c - 3 if i is None else i * SLOTS + (c - 3))
                    wh, wl, bank = WH[:, u % SPLIT, :], WL[:, u % SPLIT, :], PS[c % 4]
                    if is_tm:
                        for tt in range(TT):
                            for k in range(KT):
                                ins = product(bank[:, col(tt)], H[:, k, col(tt)], H[:, KT + k, col(tt)],
                                              wh[:, col(k)], wl[:, col(k)], k == 0, k == KT - 1)
                    else:
                        for k in range(KT):
                            ins = product(bank[:], wh[:, col(k)], wl[:, col(k)], H[:, k, :], H[:, KT + k, :],
                                          k == 0, k == KT - 1)
                    ins.then_inc(unit_used, 1)

                pe.wait_ge(*dve_done("h", name))
                for at, groups, width, is_tm in segments(name):
                    if groups > 1:
                        with pe.Fori(0, groups, 1) as i:
                            for j in range(width):
                                unit(at + j, i, is_tm)
                    else:
                        for j in range(width):
                            unit(at + j, None, is_tm)

            def mean_over_features(norm, what, source, bank, after):
                for k in range(KT):
                    pe.wait_ge(*after(k))
                    ins = mm(bank[:], cst("onesD"), source(k), start=(k == 0), stop=(k == KT - 1))
                step(ins, what, norm)

            def mean_square(norm):
                mean_over_features(norm, "ms", lambda k: tile(k), PS[7], lambda k: act_done("sq", norm, k))

            def layer_norm(norm, after):
                mean_over_features(norm, "mean", lambda k: X[:, k, :], PS[6], lambda k: after)
                mean_square(norm)

            def rope_and_attention(l):
                for t in range(5):
                    pe.wait_ge(*act_done("rsq", l, t))
                    step(mm(PS[t][:], cst("blk64"), tile(22 + t)), "rms", l, t)
                for t in range(5):
                    pe.wait_ge(*dve_done("rn", l, t))
                    step(mm(PS[t][:], cst("perm"), tile(t)), "rot", l, t)

                def scores(w):
                    hh, qt = w // 4, w % 4
                    t, s = hh // 2, 64 * (hh % 2)
                    if w == 0:
                        pe.wait_ge(*dve_done("rope", l, 4))
                    if w >= 2:
                        pe.wait_ge(*act_done("exp", l, w - 2))
                    step(mm(PS[w % 2][:], tile(Q0 + t)[s:s + 64, col(qt)], tile(K0)[s:s + 64, :]), "score", l, w)

                def turn(w):
                    hh, qt = w // 4, w % 4
                    pe.wait_ge(*dve_done("probs", l, w))
                    if w >= 2:
                        pe.wait_ge(*act_done("pT", l, w - 2))
                    for st in range(TT):
                        ins = pe.transpose(PS[2 + w % 2][:, col(st)], tile(22 + w % 2)[:, col(st)], cst("ident"))
                    step(ins, "turned", l, w)

                def values(hh):
                    t, s, pt = hh // 2, 64 * (hh % 2), 24 + 4 * (hh % 2)
                    pe.wait_ge(*act_done("pT", l, 4 * hh + 3))
                    if t >= 2 and s == 0:
                        pe.wait_ge(*dve_done("yattn", l, t - 2))
                    for st in range(TT):
                        ins = mm(PS[4 + t % 2][s:s + 64, :], tile(V0)[:, st * P + s:st * P + s + 64],
                                 tile(pt + st), start=(st == 0), stop=(st == TT - 1))
                    step(ins, "attn", l, hh)

                for w in range(34):
                    if w < 32:
                        scores(w)
                    if 1 <= w <= 32:
                        turn(w - 1)
                    if w >= 2 and (w - 2) % 4 == 3:
                        values((w - 2) // 4)

            def fourier(l):
                pe.wait_ge(consts_in, 64)
                fm = SMALL[:, SCOL["fmix"] + l * 2 * P:SCOL["fmix"] + (l + 1) * 2 * P]
                pe.wait_ge(*dve_done("yattn", l, 3))
                mm(PS[6][:, 0:2 * P], cst("c64"), fm)
                step(mm(PS[6][:, 2 * P:4 * P], cst("s64"), fm), "fmix", l)
                pe.wait_ge(*act_done("fmix", l))
                cm = tile(24).rearrange("p (a c) -> p a c", a=2)
                for tt in range(TT):
                    for j in range(2):
                        ins = mm(PS[tt].rearrange("p (a c) -> p a c", a=2)[:, :, j * P:(j + 1) * P],
                                 tile(FU0 + j)[:, col(tt)], cm[:, :, j * P:(j + 1) * P])
                    step(ins, "ft", l, tt)
                pe.wait_ge(dft_in_s, 16 * (l + 1))
                for j in range(2):
                    for tt in range(TT):
                        pe.wait_ge(*act_done("ft", l, tt))
                        mm(PS[4 + j][:], tile(25 + tt)[:, j * P:(j + 1) * P], tile(34 + tt), start=(tt == 0), stop=False)
                        ins = mm(PS[4 + j][:], tile(25 + tt)[:, (2 + j) * P:(3 + j) * P], tile(38 + tt),
                                 start=False, stop=(tt == TT - 1))
                    step(ins, "four", l, j)

            def ffn(f):
                pe.wait_ge(*dve_done("h", f))
                for q, half in enumerate(HALVES):
                    with pe.Fori(0, half // 2, 1) as i:
                        for j in range(2):
                            for w, evacuated in ((0, act_done("silu", f, q, j, i=i, lag=1)),
                                                 (1, dve_done("gated", f, q, j, i=i, lag=1))):
                                u = UNIT0[f"ffn{f}{q}"] + 2 * j + w
                                pe.wait_ge(*units(unit_split, u, i))
                                pe.wait_ge(*evacuated)
                                for k in range(KT):
                                    ins = product(PS[2 * j + w][:], WH[:, u % SPLIT, col(k)], WL[:, u % SPLIT, col(k)],
                                                  H[:, k, :], H[:, KT + k, :], k == 0, k == KT - 1)
                                ins.then_inc(unit_used, 1)
                    pe.wait_ge(*dve_done("hidden", f, q, 1))
                    n = half // 2
                    with pe.Fori(0, KT // 2, 1) as i:
                        for j in range(2):
                            pe.wait_ge(*(act_done if q == 0 else dve_done)("downed", f, q, j, i=i, lag=1))
                            for part in range(2):
                                u = UNIT0[f"down{f}{q}"] + 2 * j + part
                                pe.wait_ge(*units(unit_split, u, i))
                                for k in range(n):
                                    x = part * n + k
                                    ins = product(PS[4 + j][:], WH[:, u % SPLIT, col(k)], WL[:, u % SPLIT, col(k)],
                                                  HID[:, x, :], HID[:, 12 + x, :], x == 0, x == half - 1)
                                ins.then_inc(unit_used, 1)
                mean_square(("post", f))

            def head_norms(m):
                for h in range(4):
                    pe.wait_ge(*act_done("hsq", m, h))
                    step(mm(PS[h][:], cst("ones128"), tile(HSQ[m][h])), "hms", m, h)

            def invert(m):
                lt, xs, xts, nts, ps = INV[m[0]]
                n = LEVELS * len(lt)

                def blocks(o, left, right):
                    if m[0] == "gdn":
                        for tt in range(TT):
                            ins = mm(o[:, col(tt)], left[:, col(tt)], right[:, col(tt)])
                    else:
                        for r in (slice(0, CH), slice(CH, P)):
                            for j in range(4):
                                ins = mm(o[r, col(j, CH)], left[r, col(j, CH)], right[r, col(j, CH)])
                    return ins

                def nx(q):
                    pe.wait_ge(*dve_done("nT", m, q))
                    step(blocks(PS[3 * (q % 2)], nts[q % 2], xs[q % len(lt)]), "nx", m, q)

                nx(0)
                for q in range(n):
                    if q + 1 < n:
                        nx(q + 1)
                    if q < len(lt):
                        continue
                    h, bank = q % len(lt), 3 * (q % 2)
                    pe.wait_ge(*act_done("nx", m, q))
                    if q < n - len(lt):
                        blocks(PS[bank + 1], xts[h], ps[q % 2])
                    step(blocks(PS[bank + 2], ps[q % 2], xts[h]), "xnx", m, q)

            def linear_attention():
                m = "gla"
                pe.wait_ge(tile_copied, COPIED["mix0"] + N_EVEN)
                for j in range(2):
                    step(mm(PS[j][:], SMALL[0:16, SCOL["lora"] + j * P:SCOL["lora"] + (j + 1) * P],
                            tile(SM0)[0:16, :]), "gate", j)
                for j in range(2):
                    pe.wait_ge(*dve_done("kdec", j))
                    for tt in range(TT):
                        ins = pe.transpose(PS[2 + j][:, col(tt)], tile(33 + j)[:, col(tt)], cst("ident"))
                    step(ins, "kdT", j)
                for j in range(2):
                    pe.wait_ge(*act_done("kdT", j))
                    for odd in range(2):
                        for c in range(odd, NCH - 1, 2):
                            r, tt = CH * odd, c // 2
                            for s in range(2):
                                ins = mm(PS[4 + 2 * j + c // 4][CH * s:CH * s + CH, col(c % 4)],
                                         tile(31 + j)[r:r + CH, tt * P + CH * s:tt * P + CH * s + CH],
                                         tile(GV0 + 2 * j + s)[r:r + CH, col(tt)])
                        if not odd:
                            drain(ins)
                    step(ins, "kv", j)
                pe.wait_ge(*dve_done("kn", 1))
                for h in range(4):
                    j, s = h // 2, CH * (h % 2)
                    for tt in range(TT):
                        ins = mm(PS[h][:, col(tt)], tile(GK0 + j)[s:s + CH, col(tt)], tile(GQ0 + j)[s:s + CH, col(tt)])
                    step(ins, "gatt", h)
                pe.wait_ge(*dve_done("states"))
                for h in range(4):
                    j, s = h // 2, CH * (h % 2)
                    pe.wait_ge(*dve_done("gatt", h))
                    for tt in range(TT):
                        mm(PS[4 + h][:, col(tt)], tile(GV0 + h)[:, col(tt)], tile(GATT[h])[:, col(tt)],
                           start=(tt == 0), stop=False)
                    for c in range(1, NCH):
                        ins = mm(PS[4 + h][:, col(c, CH)], gla_state(j, c)[s:s + CH, :],
                                 tile(GQ0 + j)[s:s + CH, col(c, CH)], start=False, stop=(c == NCH - 1))
                    step(ins, "o", m, h)
                head_norms(m)

            def delta_rule():
                m = "gdn"
                pe.wait_ge(*dve_done("yh", "gla", 3))
                for t in range(8):
                    pe.wait_ge(*act_done("l2sq", t))
                    step(mm(PS[t][:], cst("ones1"), tile(13 + t)), "l2", t)
                pe.wait_ge(*act_done("rows"))
                pe.wait_ge(*dve_done("l2n", 7))
                for tt in range(TT):
                    ins = pe.transpose(PS[0][:, col(tt)], tile(22)[:, col(tt)], cst("ident"))
                step(ins, "cols")
                pe.wait_ge(*act_done("cols"))
                for h in range(4):
                    mm(PS[h][:], cst("sel", h * P, h * P + P)[DA_ROW:DA_ROW + 4, :], tile(22)[DA_ROW:DA_ROW + 4, :])
                    step(mm(PS[4 + h][:], cst("sel", h * P, h * P + P)[DB_ROW:DB_ROW + 4, :],
                            tile(22)[DB_ROW:DB_ROW + 4, :]), "rowb", h)
                for h in range(4):
                    pe.wait_ge(*dve_done("kb", h))
                    pe.wait_ge(*act_done("egb", h))
                    for tt in range(TT):
                        mm(PS[h][:, col(tt)], tile(4 + h)[:, col(tt)], tile(h)[:, col(tt)])
                    for tt in range(TT):
                        ins = mm(PS[4 + h][:, col(tt)], tile(4 + h)[:, col(tt)], tile(37 + h)[:, col(tt)])
                    step(ins, "datt", h)
                for h in range(4):
                    pe.wait_ge(*dve_done("dLT", h))
                    for tt in range(TT):
                        pe.transpose(PS[h][:, col(tt)], tile(4 + h)[:, col(tt)], cst("ident"))
                    for tt in range(TT):
                        ins = pe.transpose(PS[4 + h][:, col(tt)], tile(8 + h)[:, col(tt)], cst("ident"))
                    step(ins, "dtok", h)
                for h in range(4):
                    pe.wait_ge(*act_done("dtok", h))
                invert((m, 0))
                pe.wait_ge(*dve_done("inv", (m, 0)))
                for tt in range(TT):
                    for h in range(4):
                        ins = mm(PS[tt][:, col(h)], INV[m][2][h][:, col(tt)], tile(8 + h)[:, col(tt)])
                    step(ins, "du", tt)
                for h in range(4):
                    for tt in range(TT):
                        ins = mm(PS[4 + h][:, col(tt)], tile(37 + h)[:, col(tt)], INV[m][2][h][:, col(tt)])
                    step(ins, "dw", h)
                pe.wait_ge(*act_done("dw", 3))
                pe.wait_ge(*act_done("du", 3))
                for c in range(NCH):
                    r, tt = CH * (c % 2), c // 2
                    if c:
                        pe.wait_ge(*dve_done("dstate", c - 1))
                        for h in range(4):
                            ins = mm(PS[0][:, col(h)], INV[m][1][h][:, col(tt)], STATE[:, col(h)])
                        step(ins, "dws", c)
                        for h in range(4):
                            mm(PS[4 + h][:, col(c, CH)], STATE[:, col(h)], tile(13 + h)[:, col(c, CH)],
                               start=(c == 1), stop=False)
                    pe.wait_ge(*dve_done("dv", c))
                    if c < NCH - 1:
                        for h in range(4):
                            ins = mm(PS[1][:, col(h)], tile(29 + h)[r:r + CH, col(tt)], tile(8 + tt)[r:r + CH, col(h)])
                        step(ins, "dupd", c)
                    if c % 2:
                        for h in range(4):
                            ins = mm(PS[4 + h][:, col(tt)], tile(8 + tt)[:, col(h)], tile(h)[:, col(tt)],
                                     start=False, stop=(tt == TT - 1))
                            if tt == TT - 1:
                                step(ins, "o", m, h)
                head_norms(m)

            def lru():
                for j in range(4):
                    pe.wait_ge(*dve_done("lconv", j))
                    mm(PS[j][:], SMALL[:, SCOL["lwa"] + j * P:SCOL["lwa"] + (j + 1) * P], tile(22 + j))
                    step(mm(PS[4 + j][:], SMALL[:, SCOL["lwx"] + j * P:SCOL["lwx"] + (j + 1) * P], tile(22 + j)),
                         "lgate", j)

            def rwkv():
                pe.wait_ge(*act_done("rlora"))
                pe.wait_ge(*act_done("lgate", 3))
                wa2 = SMALL[:, SCOL["wa2"]:SCOL["wa2"] + 4 * P]
                for j in range(4):
                    mm(PS[j][:], wa2[0:64, col(j)], tile(WA0)[0:64, :])
                    step(mm(PS[4 + j][:], wa2[64:128, col(j)], tile(WA0)[64:128, :]), "rlora", j)
                for j in range(4):
                    pe.wait_ge(*act_done("kksq", j))
                    step(mm(PS[j][:], cst("blk1"), tile(40 + j)), "kk2", j)
                for j in range(4):
                    pe.wait_ge(*dve_done("bonus0", j))
                    step(mm(PS[4 + j][:], cst("blk1"), tile(14 + j)), "bonus", j)
                pe.wait_ge(*dve_done("rprep"))
                for tt in range(TT):
                    m = ("rwkv", tt)
                    if tt:
                        pe.wait_ge(*act_done("ry", tt - 1))
                        pe.wait_ge(*dve_done("rstate", 2 * tt - 1))
                    for q in range(4):
                        for j in range(4):
                            ins = pe.transpose(PS[q][:, col(j)], tile((24, 8, 28, 18)[q] + j)[:, col(tt)], cst("ident"))
                        step(ins, "rtok", tt, q)

                    def pairs(bank, left, right):
                        for c in (2 * tt, 2 * tt + 1):
                            r = CH * (c % 2)
                            for h in range(8):
                                j, s = h // 2, 64 * (h % 2)
                                ins = mm(PS[bank + h % 2][r:r + CH, col(j, CH)], tile(left + j)[s:s + 64, col(c, CH)],
                                         tile(right + j)[s:s + 64, col(c, CH)])
                        return ins

                    pairs(4, 36, 24)
                    step(pairs(6, 4, 24), "rmat", tt)
                    pe.wait_ge(*dve_done("rmat", tt))
                    for q in range(4):
                        pe.wait_ge(*act_done("rtok", tt, q))
                    for r in (slice(0, CH), slice(CH, P)):
                        for h in range(8):
                            ins = mm(PS[0][r, hc(h)], RT["aak"][r, hc(h)], RT["v"][r, hc(h)])
                    step(ins, "rz", tt)
                    pe.wait_ge(*act_done("rz", tt))
                    invert(m)
                    pe.wait_ge(*dve_done("inv", m))
                    xt = tile(35)
                    for r in (slice(0, CH), slice(CH, P)):
                        for h in range(8):
                            ins = mm(PS[0][r, hc(h)], xt[r, hc(h)], RT["z"][r, hc(h)])
                    step(ins, "ru", tt)
                    for odd, r in enumerate((slice(0, CH), slice(CH, P))):
                        for h in range(8):
                            j, s = h // 2, 64 * (h % 2)
                            ins = mm(PS[1 + odd][s:s + 64, col(j, CH)], RT["a"][r, hc(h)], xt[r, hc(h)])
                    step(ins, "rw", tt)
                    pairs(4, 36, 0)
                    step(pairs(6, 4, 0), "rout", tt)
                    pe.wait_ge(*act_done("rw", tt))
                    pe.wait_ge(*dve_done("rout", tt))
                    started = set()
                    for c in (2 * tt, 2 * tt + 1):
                        odd = c % 2
                        r = slice(CH * odd, CH * odd + CH)
                        if c:
                            pe.wait_ge(*dve_done("rstate", c - 1))
                            for h in range(8):
                                j, s = h // 2, 64 * (h % 2)
                                ins = mm(PS[3 + h % 2][r, col(j, 64)],
                                         RT["w"][s:s + 64, odd * 256 + j * 64:odd * 256 + j * 64 + 64],
                                         STATE[s:s + 64, col(j, 64)])
                            step(ins, "rws", c)
                            for h in range(8):
                                j, s = h // 2, 64 * (h % 2)
                                ins = mm(PS[2][s:s + 64, j * P + CH * odd:j * P + CH * odd + CH],
                                         STATE[s:s + 64, col(j, 64)], tile(j)[s:s + 64, col(c, CH)],
                                         start=(s not in started), stop=False)
                                started.add(s)
                            drain(ins)
                        pe.wait_ge(*dve_done("ruc", c))
                        if c < NCH - 1:
                            for h in range(8):
                                j, s = h // 2, 64 * (h % 2)
                                mm(PS[1][s:s + 64, col(j, 64)], RT["bd"][r, hc(h)], RT["z"][r, hc(h)],
                                   start=True, stop=False)
                                ins = mm(PS[1][s:s + 64, col(j, 64)], RT["kd"][r, hc(h)], RT["v"][r, hc(h)],
                                         start=False, stop=True)
                            step(ins, "rupd", c)
                        for h in range(8):
                            j, s = h // 2, 64 * (h % 2)
                            y = PS[2][s:s + 64, j * P + CH * odd:j * P + CH * odd + CH]
                            mm(y, RT["z"][r, hc(h)], RT["rb"][r, hc(h)], start=(s not in started), stop=False)
                            started.add(s)
                            ins = mm(y, RT["v"][r, hc(h)], RT["rk"][r, hc(h)], start=False, stop=(odd == 1))
                        drain(ins)
                    step(mm(PS[5][0:1, 0:1], cst("ident")[:, 0:1], cst("ident")[:, 0:1]), "ry", tt)
                pe.wait_ge(*act_done("ry", TT - 1))
                for j in range(4):
                    step(mm(PS[j][:], cst("blk64"), tile(j)), "gmean", j)
                for j in range(4):
                    pe.wait_ge(*act_done("gsq", j))
                    step(mm(PS[4 + j][:], cst("blk64"), tile(22 + j)), "gvar", j)
                for j in range(4):
                    pe.wait_ge(*dve_done("gcentred", j))
                    step(mm(PS[j][:], SMALL[:, SCOL["g2"] + j * P:SCOL["g2"] + (j + 1) * P], tile(GL0)), "gout", j)

            pe.wait_ge(consts_in, 64)
            for q in range(6):
                modulation(q)
                if q:
                    modulation_columns(q - 1)
            modulation_columns(5)
            for l in range(DEPTH):
                layer_norm(("ln", l), dve_done("x", "first", l - 1) if l else (consts_in, 64))
                project(f"first{l}")
                rope_and_attention(l)
                fourier(l)
                project(f"firstout{l}")
                layer_norm(("pln", l), dve_done("res", l))
            for i in range(DEPTH):
                mean_square(("pre", f"{i}0"))
                ffn(f"{i}0")
                mean_square(("pre", f"mix{i}"))
                project(f"mix{i}")
                if i % 2 == 0:
                    linear_attention()
                    delta_rule()
                else:
                    lru()
                    rwkv()
                project(f"mixout{i}")
                mean_square(("post", f"mix{i}"))
                mean_square(("pre", f"{i}1"))
                ffn(f"{i}1")

        @block.scalar
        def _(act):
            def a(o, i, func, *name, bias=0.0, scale=1.0, chain=True, accum=None):
                extra = {} if accum is None else {"accum_out": accum}
                ins = nc.scalar.activation(o, i, func, bias=bias, scale=scale, **extra)
                ins.then_inc(*act_signal((name if len(name) > 1 else name[0]) if name else None))
                if chain:
                    act.wait_ge(*act_so_far())

            def squares(norm, source, after):
                for k in range(KT):
                    act.wait_ge(*after(k))
                    a(tile(k), source(k), ACT.Square, "sq", norm, k, chain=False)
                act.wait_ge(*pe_done("ms", norm))
                a(RSTD[:, 0, :], PS[7][:], ACT.Sqrt, "sd", norm, bias=v("eps5" if norm[0] in ("ln", "pln") else "eps6"))

            def high(u, i=None):
                act.wait_ge(*loaded(u, i))
                if u >= SPLIT:
                    act.wait_ge(*units(unit_used, u - SPLIT, i))
                nc.scalar.activation(WH[:, u % SPLIT, :], RING[:, u % SLOTS, :], ACT.Copy).then_inc(unit_high, 1)

            def split_tiles(name, source, after=None):
                for k in range(KT):
                    act.wait_ge(*(after or dve_done("t", name, k)))
                    a(H[:, k, :], source(k), ACT.Copy, "t", name, k, chain=False)

            def project(name, dest):
                def unit(j, i):
                    c = COPIED[name] + j
                    high(UNIT0[name] + j + SPLIT, i)
                    at = dest + j if i is None else i * SLOTS + (dest + j)
                    nc.scalar.activation(BIG[:, bass.ds(at, 1), :], PS[c % 4][:].unsqueeze(1),
                                         ACT.Copy).then_inc(tile_copied, 1)

                for at, groups, width, _ in segments(name):
                    if groups > 1:
                        with act.Fori(0, groups, 1) as i:
                            for j in range(width):
                                unit(at + j, i)
                    else:
                        for j in range(width):
                            unit(at + j, None)
                count = dict((n, c) for n, c, _ in STREAM)[name]
                act.wait_ge(tile_copied, COPIED[name] + count)

            def rope_and_attention(l):
                for t in range(5):
                    a(tile(22 + t), tile(t), ACT.Square, "rsq", l, t, chain=False)
                for t in range(5):
                    act.wait_ge(*pe_done("rms", l, t))
                    a(tile(22 + t), PS[t][:], ACT.Sqrt, "rsd", l, t, bias=v("eps6"))
                for t0, n in ((GA0, 4), (GC0, 2), (GF0, 2)):
                    a(BIG[:, t0:t0 + n, :], BIG[:, t0:t0 + n, :], ACT.Silu, "gates", l, t0)
                for w in range(33):
                    if w < 32:
                        act.wait_ge(*dve_done("negmax", l, w))
                        if w >= 2:
                            act.wait_ge(*pe_done("turned", l, w - 2))
                        a(tile(22 + w % 2), PS[w % 2][:], ACT.Exp, "exp", l, w, bias=STAT[:, 1, w:w + 1],
                          scale=0.125, accum=STAT[:, 2, w:w + 1], chain=False)
                    if w:
                        u = w - 1
                        hh = u // 4
                        act.wait_ge(*pe_done("turned", l, u))
                        if hh >= 2:
                            act.wait_ge(*pe_done("attn", l, hh - 2))
                        pt = 24 + 4 * (hh % 2)
                        a(BIG[:, pt:pt + 4, col(u % 4)], by_tt(PS[2 + u % 2][:]), ACT.Copy, "pT", l, u, chain=False)

            def fourier(l):
                act.wait_ge(*pe_done("fmix", l))
                a(tile(24), PS[6][:], ACT.Copy, "fmix", l, chain=False)
                for tt in range(TT):
                    act.wait_ge(*pe_done("ft", l, tt))
                    a(tile(25 + tt), PS[tt][:], ACT.Copy, "ft", l, tt, chain=False)

            def ffn(f):
                for q, half in enumerate(HALVES):
                    up, down = UNIT0[f"ffn{f}{q}"], UNIT0[f"down{f}{q}"]
                    first = act_begin_loop()
                    with act.Fori(0, half // 2, 1) as i:
                        for j in range(2):
                            high(up + 2 * j + SPLIT, i)
                            act.wait_ge(*dve_done("gated", f, q, j, i=i, lag=1))
                            a(GATE[:, j, :], PS[2 * j][:], ACT.Silu, "silu", f, q, j, chain=False)
                            high(up + 2 * j + 1 + SPLIT, i)
                            act.wait_ge(*dve_done("gated", f, q, j, i=i))
                            a(HID[:, bass.ds(i * 2 + j, 1), :], GATE[:, 2 + j:3 + j, :], ACT.Copy, "hidden", f, q, j,
                              chain=False)
                    act_end_loop(first, half // 2)
                    first = act_begin_loop()
                    with act.Fori(0, KT // 2, 1) as i:
                        for j in range(2):
                            high(down + 2 * j + SPLIT, i)
                            high(down + 2 * j + 1 + SPLIT, i)
                            if q == 0:
                                a(BIG[:, bass.ds(i * 2 + (24 + j), 1), :], PS[4 + j][:].unsqueeze(1), ACT.Copy,
                                  "downed", f, q, j, chain=False)
                    act_end_loop(first, KT // 2)
                squares(("post", f), lambda k: tile(24 + k), lambda k: dve_done("downed", f, 1, 1))

            def head_norms(m, bank):
                for h in range(4):
                    act.wait_ge(*pe_done("o", m, h))
                    a(tile(HSQ[m][h]), PS[bank + h][:], ACT.Square, "hsq", m, h, chain=False)
                for h in range(4):
                    act.wait_ge(*pe_done("hms", m, h))
                    a(tile(HSQ[m][h]), PS[h][:], ACT.Sqrt, "hsd", m, h, bias=v("eps6"), chain=False)

            def invert(m):
                lt, _, _, _, ps = INV[m[0]]
                for q in range(len(lt), LEVELS * len(lt)):
                    act.wait_ge(*pe_done("nx", m, q))
                    a(ps[q % 2], PS[3 * (q % 2)][:, 0:ps[0].shape[1]], ACT.Copy, "nx", m, q, chain=False)

            def softplus_part(o, x):
                a(o, x, ACT.Abs)
                a(o, o, ACT.Exp, scale=-1.0)

            def linear_attention():
                for j in range(2):
                    act.wait_ge(*pe_done("gate", j))
                    a(tile(29 + j), PS[j][:], ACT.Identity, bias=v("lorab", j))
                    softplus_part(tile(31 + j), tile(29 + j))
                for j in range(2):
                    a(tile(31 + j), tile(31 + j), ACT.Ln, "lsig", j, bias=v("one"))
                for j in range(2):
                    act.wait_ge(*dve_done("dl", j))
                    a(tile(35 + j), tile(31 + j), ACT.Exp, scale=1 / 16)
                    a(tile(29 + j), tile(31 + j), ACT.Exp, scale=-1 / 16)
                    a(tile(33 + j), tile(33 + j), ACT.Exp, "gexp", j, scale=1 / 16)
                a(BIG[:, GG0:GG0 + 4, :], BIG[:, GG0:GG0 + 4, :], ACT.Silu, "ggate")
                for j in range(2):
                    act.wait_ge(*pe_done("kdT", j))
                    a(tile(31 + j), PS[2 + j][:], ACT.Copy, "kdT", j)
                head_norms("gla", 4)

            def delta_rule():
                for t in range(12):
                    act.wait_ge(*dve_done("dconv", t))
                    a(tile(t), tile(t), ACT.Silu, "dconv", t)
                a(BIG[:, DZ0:DZ0 + 4, :], BIG[:, DZ0:DZ0 + 4, :], ACT.Silu, "zgate")
                for t in range(8):
                    a(tile(13 + t), tile(t), ACT.Square, "l2sq", t, chain=False)
                g, b = slice(DA_ROW, DA_ROW + 4), slice(DB_ROW, DB_ROW + 4)
                a(tile(SM0)[g], tile(SM0)[g], ACT.Identity, bias=v("dtb")[g])
                softplus_part(tile(21)[g], tile(SM0)[g])
                a(STAT[g, 0, 0:1], v("alog")[g], ACT.Exp)
                a(tile(21)[g], tile(21)[g], ACT.Ln, "dsp", bias=v("one")[g])
                act.wait_ge(*dve_done("rows0"))
                a(tile(22)[b], tile(SM0)[b], ACT.Sigmoid, "beta")
                for t in range(8):
                    act.wait_ge(*pe_done("l2", t))
                    a(tile(13 + t), PS[t][:], ACT.Sqrt, "l2sd", t, bias=v("eps6"), chain=False)
                act.wait_ge(*dve_done("gc"))
                a(tile(22)[EG_ROW:EG_ROW + 4], tile(22)[g], ACT.Exp)
                e = slice(ED_ROW, ED_ROW + 4)
                a(tile(22)[e], tile(22)[e], ACT.Exp, "rows")
                act.wait_ge(*pe_done("cols"))
                a(tile(23), PS[0][:], ACT.Copy, "cols")
                for h in range(4):
                    act.wait_ge(*pe_done("rowb", h))
                    a(tile(33 + h), PS[h][:], ACT.Exp, "egb", h, chain=False)
                    act.wait_ge(*dve_done("ddec", h))
                    a(tile(29 + h), tile(29 + h), ACT.Exp, "ddec", h)
                act.wait_ge(*dve_done("colbe"))
                for h in range(4):
                    act.wait_ge(*pe_done("dtok", h))
                    for tt in range(TT):
                        c = tt * P + h
                        cols = tile(23)
                        a(tile(37 + h)[:, col(tt)], PS[h][:, col(tt)], ACT.Copy, scale=STAT[:, 1, 4 * tt + h:4 * tt + h + 1],
                          chain=False)
                        a(tile(29 + h)[:, col(tt)], PS[h][:, col(tt)], ACT.Copy,
                          scale=cols[:, c + ED_ROW:c + ED_ROW + 1], chain=False)
                    for tt in range(TT):
                        c = tt * P + h
                        last = dict(chain=False)
                        name = ("dtok", h) if tt == TT - 1 else ()
                        a(tile(8 + h)[:, col(tt)], PS[4 + h][:, col(tt)], ACT.Copy, *name,
                          scale=tile(23)[:, c + DB_ROW:c + DB_ROW + 1], **last)
                invert(("gdn", 0))
                for tt in range(TT):
                    act.wait_ge(*pe_done("du", tt))
                    a(tile(17 + tt), PS[tt][:], ACT.Copy, "du", tt, chain=False)
                for h in range(4):
                    act.wait_ge(*pe_done("dw", h))
                    a(INV["gdn"][1][h], PS[4 + h][:], ACT.Copy, "dw", h, chain=False)
                head_norms("gdn", 4)

            def lru():
                act.wait_ge(consts_in, 64)
                a(LRUV[:, 0:4], v4("lam"), ACT.Abs)
                a(LRUV[:, 0:4], LRUV[:, 0:4], ACT.Exp, "lam", scale=-1.0)
                for j in range(4):
                    act.wait_ge(*pe_done("lgate", j))
                    a(tile(26 + j), PS[j][:], ACT.Sigmoid, bias=v("lba", j), chain=False)
                    a(tile(30 + j), PS[4 + j][:], ACT.Sigmoid, "lgate", j, bias=v("lbx", j))
                act.wait_ge(*dve_done("lam"))
                for j in range(4):
                    a(tile(34 + j), tile(26 + j), ACT.Exp, scale=LRUV[:, 8 + j:9 + j], chain=False)
                    a(tile(26 + j), tile(26 + j), ACT.Tanh, "ltanh", j, scale=LRUV[:, 12 + j:13 + j])
                for j in range(4):
                    act.wait_ge(*dve_done("gelu0", j))
                    a(tile(14 + j), tile(14 + j), ACT.Tanh, "gelu", j, scale=float(np.sqrt(2 / np.pi)), chain=False)
                for j in range(4):
                    act.wait_ge(*dve_done("lmult", j))
                    a(tile(38 + j), tile(38 + j), ACT.Sqrt, "lmult", j, chain=False)

            def rwkv():
                act.wait_ge(*dve_done("shift", WA0))
                a(tile(WA0)[0:64], tile(WA0)[0:64], ACT.Tanh)
                act.wait_ge(*dve_done("shift", GL0))
                a(tile(GL0), tile(GL0), ACT.Sigmoid, "rlora")
                act.wait_ge(*dve_done("shift", WA0 - 1))
                for j in range(4):
                    act.wait_ge(*pe_done("rlora", j))
                    a(tile(24 + j), PS[j][:], ACT.Sigmoid, bias=v("w0", j), chain=False)
                    a(tile(28 + j), PS[4 + j][:], ACT.Sigmoid, "rgate", j, bias=v("a0", j), chain=False)
                for j in range(4):
                    act.wait_ge(*dve_done("kk", j))
                    a(tile(40 + j), tile(36 + j), ACT.Square, "kksq", j, chain=False)
                for j in range(4):
                    act.wait_ge(*pe_done("kk2", j))
                    a(tile(40 + j), PS[j][:], ACT.Sqrt, "kksd", j, bias=v("eps6"), chain=False)
                for j in range(4):
                    act.wait_ge(*dve_done("rcum", j))
                    a(tile(24 + j), tile(24 + j), ACT.Exp, scale=-DECAY, chain=False)
                    a(tile(32 + j), tile(40 + j), ACT.Exp, scale=-DECAY)
                    a(tile(40 + j), tile(40 + j), ACT.Exp, scale=DECAY, chain=False)
                    a(tile(18 + j), tile(18 + j), ACT.Exp, "rexp", j, scale=-DECAY, chain=False)
                for tt in range(TT):
                    m = ("rwkv", tt)
                    for q, name in enumerate(("a", "v", "bd", "kd")):
                        act.wait_ge(*pe_done("rtok", tt, q))
                        a(RT[name].rearrange("p (g j i) -> p g j i", g=2, j=4),
                          PS[q][:].rearrange("p (j g i) -> p g j i", g=2, j=4), ACT.Copy, "rtok", tt, q, chain=False)
                    act.wait_ge(*pe_done("rz", tt))
                    a(RT["z"], PS[0][:], ACT.Copy, "rz", tt)
                    invert(m)
                    act.wait_ge(*pe_done("ru", tt))
                    a(RT["z"], PS[0][:], ACT.Copy, "ru", tt)
                    act.wait_ge(*pe_done("rw", tt))
                    for odd in range(2):
                        a(RT["w"][:, 256 * odd:256 * odd + 256], PS[1 + odd][:, 0:256], ACT.Copy,
                          *(("rw", tt) if odd else ()))
                    act.wait_ge(*pe_done("ry", tt))
                    a(BIG[:, 0:4, col(tt)], by_tt(PS[2][:]), ACT.Copy, "ry", tt)
                for j in range(4):
                    act.wait_ge(*dve_done("gcentred", j))
                    a(tile(22 + j), tile(j), ACT.Square, "gsq", j, chain=False)
                for j in range(4):
                    act.wait_ge(*pe_done("gvar", j))
                    a(tile(22 + j), PS[4 + j][:], ACT.Sqrt, "gsd", j, bias=v("epsg"), chain=False)

            act.wait_ge(consts_in, 64)
            for u in range(SPLIT):
                high(u)
            for l in range(DEPTH):
                squares(("ln", l), lambda k: tile(8 + k), lambda k: dve_done("xc", ("ln", l), k))
                split_tiles(f"first{l}", lambda k: tile(8 + k))
                project(f"first{l}", 0)
                rope_and_attention(l)
                fourier(l)
                split_tiles(f"firstout{l}", lambda k: tile(Y_FIRST[k]), dve_done("four", l, 1))
                project(f"firstout{l}", 24)
                squares(("pln", l), lambda k: tile(8 + k), lambda k: dve_done("xc", ("pln", l), k))
            for i in range(DEPTH):
                ready = dve_done("x", "first", 1) if i == 0 else dve_done("x", "11" if i == 2 else "01")
                squares(("pre", f"{i}0"), lambda k: X[:, k, :], lambda k: ready)
                split_tiles(f"{i}0", lambda k: tile(8 + k))
                ffn(f"{i}0")
                squares(("pre", f"mix{i}"), lambda k: X[:, k, :], lambda k: dve_done("x", f"{i}0"))
                split_tiles(f"mix{i}", lambda k: tile(8 + k))
                project(f"mix{i}", 0)
                if i % 2 == 0:
                    linear_attention()
                    delta_rule()
                else:
                    lru()
                    rwkv()
                split_tiles(f"mixout{i}", lambda k: tile(Y_MIX[i][k]), None if i % 2 else dve_done("yh", "gdn", 3))
                project(f"mixout{i}", 24)
                squares(("post", f"mix{i}"), lambda k: tile(24 + k), lambda k: (tile_copied, COPIED[f"mixout{i}"] + KT))
                squares(("pre", f"{i}1"), lambda k: X[:, k, :], lambda k: dve_done("x", f"mix{i}"))
                split_tiles(f"{i}1", lambda k: tile(8 + k))
                ffn(f"{i}1")

        @block.vector
        def _(dve):
            ve = nc.vector

            def d(ins, *name, chain=True, pair=False):
                ins.then_inc(*dve_signal((name if len(name) > 1 else name[0]) if name else None))
                steps, value = dve_so_far()
                if pair:
                    dve.wait_ge(steps, value - 1)
                elif chain:
                    dve.wait_ge(steps, value)

            def stt(o, a, s, b, op0, op1):
                return ve.scalar_tensor_tensor(out=o, in0=a, scalar=s, in1=b, op0=op0, op1=op1)

            def reciprocal_std(norm):
                dve.wait_ge(*act_done("sd", norm))
                d(ve.reciprocal(RSTD[:, 1, :], RSTD[:, 0, :]))

            def low(u, i=None):
                dve.wait_ge(*units(unit_high, u, i))
                if u >= SPLIT:
                    dve.wait_ge(*units(unit_used, u - SPLIT, i))
                ve.tensor_tensor(WL[:, u % SPLIT, :], RING[:, u % SLOTS, :], WH[:, u % SPLIT, :].bitcast(F32),
                                 ALU.subtract).then_inc(unit_split, 1)

            def lows(name):
                count = dict((n, c) for n, c, _ in STREAM)[name]
                u, groups = UNIT0[name] + SPLIT, count // SLOTS
                if groups:
                    with dve.Fori(0, groups, 1) as i:
                        for j in range(SLOTS):
                            low(u + j, i)
                for j in range(groups * SLOTS, count):
                    low(u + j)

            def split_tiles(name, source):
                for k in range(KT):
                    dve.wait_ge(*act_done("t", name, k))
                    d(ve.tensor_tensor(H[:, KT + k, :], source(k), H[:, k, :].bitcast(F32), ALU.subtract),
                      *(("h", name) if k == KT - 1 else ()), chain=(k == 3))

            def layer_norm(norm, l, first):
                dve.wait_ge(*pe_done("mean", norm))
                for k in range(KT):
                    d(ve.tensor_tensor(tile(8 + k), X[:, k, :], PS[6][:], ALU.subtract), "xc", norm, k, chain=False)
                reciprocal_std(norm)
                for k in range(KT):
                    last = k == KT - 1
                    if first:
                        d(ve.tensor_tensor(tile(8 + k), tile(8 + k), RSTD[:, 1, :], ALU.mult), chain=last)
                    else:
                        d(stt(X[:, k, :], tile(8 + k), v("lng", 8 * l + k), RSTD[:, 1, :], ALU.mult, ALU.mult), chain=last)
                for k in range(KT):
                    last = k == KT - 1
                    if first:
                        d(ve.tensor_scalar(tile(8 + k), tile(8 + k), MOD[:, l, 8 + k:9 + k], MOD[:, l, k:k + 1],
                                           ALU.mult, ALU.add), "t", f"first{l}", k, chain=last)
                    else:
                        d(ve.tensor_scalar(X[:, k, :], X[:, k, :], v("lnb", 8 * l + k), None, ALU.add),
                          *(("x", "first", l) if last else ()), chain=last)
                if first:
                    split_tiles(f"first{l}", lambda k: tile(8 + k))

            def pre_norm(name, w):
                reciprocal_std(("pre", name))
                for k in range(KT):
                    d(stt(tile(8 + k), X[:, k, :], v("nw", w * 8 + k), RSTD[:, 1, :], ALU.mult, ALU.mult),
                      "t", name, k, chain=(k == KT - 1))
                split_tiles(name, lambda k: tile(8 + k))

            def post_norm(name, w, factor):
                reciprocal_std(("post", name))
                for k in range(KT):
                    d(stt(tile(24 + k), tile(24 + k), v("nw", w * 8 + k), RSTD[:, 1, :], ALU.mult, ALU.mult),
                      chain=(k == KT - 1))
                for k in range(KT):
                    d(stt(X[:, k, :], tile(24 + k), factor, X[:, k, :], ALU.mult, ALU.add),
                      *(("x", name) if k == KT - 1 else ()), chain=(k == KT - 1))

            def modulation():
                dve.wait_ge(consts_in, 64)
                for q in range(6):
                    dve.wait_ge(*pe_done("modrow", q))
                    if q >= 2:
                        dve.wait_ge(*pe_done("mod", q - 2))
                    for side in range(2):
                        d(ve.tensor_copy(GATE[0:1, 2 * (q % 2) + side, :], PS[2 * (q % 3) + side][0:1, :]),
                          *(("modrow", q) if side else ()), chain=False)
                dve.wait_ge(*pe_done("mod", 5))
                d(ve.tensor_tensor(MOD[:].rearrange("p l n -> p (l n)"), PS[7][:, 0:48],
                                   VEC[:, VCOL["bada"]:VCOL["bada"] + 48], ALU.add))
                d(ve.tensor_scalar(MOD[:, :, 8:24], MOD[:, :, 8:24], 1.0, None, ALU.add))

            def rope_and_attention(l):
                dve.wait_ge(tile_copied, COPIED[f"first{l}"] + N_FIRST)
                for t in range(5):
                    dve.wait_ge(*act_done("rsd", l, t))
                    d(ve.reciprocal(tile(22 + t), tile(22 + t)))
                    gain = v("kg", l) if t == K0 else v("qg", l)
                    d(stt(tile(t), tile(t), gain, tile(22 + t), ALU.mult, ALU.mult), "rn", l, t)
                for t in range(5):
                    dve.wait_ge(*pe_done("rot", l, t))
                    d(ve.tensor_tensor(tile(22 + t), PS[t][:], cst("sin"), ALU.mult), chain=False)
                    d(ve.tensor_tensor(tile(t), tile(t), cst("cos"), ALU.mult))
                    d(ve.tensor_tensor(tile(t), tile(t), tile(22 + t), ALU.add), "rope", l, t)
                for w in range(34):
                    if w < 32:
                        dve.wait_ge(*pe_done("score", l, w))
                        d(ve.reduce_max(STAT[:, 0, w:w + 1], PS[w % 2][:], AX_X))
                        d(ve.tensor_scalar(STAT[:, 1, w:w + 1], STAT[:, 0, w:w + 1], -0.125, None, ALU.mult),
                          "negmax", l, w, chain=False)
                    if 1 <= w <= 32:
                        u = w - 1
                        dve.wait_ge(*act_done("exp", l, u))
                        d(ve.reciprocal(STAT[:, 3, u:u + 1], STAT[:, 2, u:u + 1]))
                        d(ve.tensor_scalar(tile(22 + u % 2), tile(22 + u % 2), STAT[:, 3, u:u + 1], None, ALU.mult),
                          "probs", l, u)
                    if w >= 9 and (w - 9) % 8 == 0 or w == 33:
                        t = (w - 9) // 8
                        if t < 4:
                            dve.wait_ge(*pe_done("attn", l, 2 * t + 1))
                            dve.wait_ge(*act_done("gates", l, GF0))
                            d(ve.tensor_tensor(tile(t), PS[4 + t % 2][:], tile(GA0 + t), ALU.mult), "yattn", l, t)

            def short_conv(l):
                for j in range(2):
                    u, y, w = tile(32 + j), tile(Y_FIRST[4 + j]), 6 * l + j
                    d(ve.tensor_tensor(u, tile(CC0 + j), tile(CU0 + j), ALU.mult))
                    d(ve.tensor_scalar(y, u, v("cw", w + 2), None, ALU.mult))
                    d(stt(y[:, 1:T], u[:, 0:T - 1], v("cw", w), y[:, 1:T], ALU.mult, ALU.add))
                    d(stt(y[:, 0:T - 1], u[:, 1:T], v("cw", w + 4), y[:, 0:T - 1], ALU.mult, ALU.add))
                    d(ve.tensor_tensor(y, y, tile(CB0 + j), ALU.mult))
                    d(ve.tensor_tensor(y, y, tile(GC0 + j), ALU.mult))

            def residual(l):
                dve.wait_ge(tile_copied, COPIED[f"firstout{l}"] + KT)
                for k in range(KT):
                    d(ve.tensor_scalar(tile(24 + k), tile(24 + k), MOD[:, l, 16 + k:17 + k], None, ALU.mult),
                      chain=(k == KT - 1))
                for k in range(KT):
                    d(stt(X[:, k, :], X[:, k, :], ALPHA, tile(24 + k), ALU.mult, ALU.add),
                      *(("res", l) if k == KT - 1 else ()), chain=(k == KT - 1))

            def ffn(f):
                for q, half in enumerate(HALVES):
                    up, down = UNIT0[f"ffn{f}{q}"], UNIT0[f"down{f}{q}"]
                    first = dve_begin_loop()
                    with dve.Fori(0, half // 2, 1) as i:
                        for j in range(2):
                            low(up + 2 * j + SPLIT, i)
                            low(up + 2 * j + 1 + SPLIT, i)
                            dve.wait_ge(*act_done("silu", f, q, j, i=i))
                            dve.wait_ge(*act_done("hidden", f, q, j, i=i, lag=1))
                            d(ve.tensor_tensor(GATE[:, 2 + j, :], GATE[:, j, :], PS[2 * j + 1][:], ALU.mult),
                              "gated", f, q, j, chain=False)
                            dve.wait_ge(*act_done("hidden", f, q, j, i=i))
                            dve.wait_ge(*dve_done("gated", f, q, j, i=i))
                            d(ve.tensor_tensor(HID[:, bass.ds(i * 2 + (12 + j), 1), :], GATE[:, 2 + j:3 + j, :],
                                               HID[:, bass.ds(i * 2 + j, 1), :].bitcast(F32), ALU.subtract),
                              "hidden", f, q, j, chain=False)
                    dve_end_loop(first, half // 2)
                    first = dve_begin_loop()
                    with dve.Fori(0, KT // 2, 1) as i:
                        for j in range(2):
                            low(down + 2 * j + SPLIT, i)
                            low(down + 2 * j + 1 + SPLIT, i)
                            if q == 1:
                                at = bass.ds(i * 2 + (24 + j), 1)
                                d(ve.tensor_tensor(BIG[:, at, :], PS[4 + j][:].unsqueeze(1), BIG[:, at, :], ALU.add),
                                  "downed", f, q, j, chain=False)
                    dve_end_loop(first, KT // 2)

            def head_norms(m, bank, ys, gain, gate0):
                for h in range(4):
                    dve.wait_ge(*act_done("hsd", m, h))
                    r = tile(HSQ[m][h])
                    d(ve.reciprocal(r, r))
                    d(stt(r, PS[bank + h][:], gain, r, ALU.mult, ALU.mult))
                    d(ve.tensor_tensor(tile(ys[h]), r, tile(gate0 + h), ALU.mult), "yh", m, h)

            def invert(m):
                lt, xs, xts, nts, _ = INV[m[0]]
                n, b = LEVELS * len(lt), len(lt)
                width = lt[0].shape[1]

                def mask(name):
                    return mask4(name) if m[0] == "gdn" else mask_chunks(name)

                def by4(ap):
                    return ap.rearrange("p (t c) -> p t c", t=4)

                for h in range(b):
                    d(ve.tensor_copy(by4(xs[h]), mask("ident")), chain=False)
                    d(ve.tensor_copy(by4(xts[h]), mask("ident")))

                def update(q):
                    h, bank = q % b, 3 * (q % 2)
                    if q < b:
                        dve.wait_ge(*pe_done("nx", m, q))
                        d(ve.tensor_tensor(xs[h], xs[h], PS[bank][:, 0:width], ALU.subtract), chain=False)
                        d(ve.tensor_tensor(xts[h], xts[h], nts[q % 2], ALU.subtract))
                        return
                    dve.wait_ge(*pe_done("xnx", m, q))
                    if q < n - b:
                        d(ve.tensor_tensor(xs[h], xs[h], PS[bank + 1][:, 0:width], ALU.subtract), chain=False)
                    d(ve.tensor_tensor(xts[h], xts[h], PS[bank + 2][:, 0:width], ALU.subtract),
                      *(("inv", m) if q == n - 1 else ()))

                for q in range(n):
                    d(ve.tensor_tensor(by4(nts[q % 2]), by4(lt[q % b]), mask(f"lev{q // b}"), ALU.mult), "nT", m, q)
                    if q:
                        update(q - 1)
                update(n - 1)

            def linear_attention():
                dve.wait_ge(tile_copied, COPIED["mix0"] + N_EVEN)
                for j in range(2):
                    dve.wait_ge(*act_done("lsig", j))
                    d(stt(tile(29 + j), tile(29 + j), 0.0, tile(31 + j), ALU.min, ALU.subtract))
                    d(ve.tensor_tensor_scan(tile(31 + j), cst("reset"), tile(29 + j), 0.0, ALU.mult, ALU.add))
                    b = by_chunk(tile(31 + j))
                    d(ve.tensor_tensor(by_chunk(tile(33 + j)), b[:, :, CH - 1:CH].broadcast_to([P, NCH, CH]), b,
                                       ALU.subtract), "dl", j)
                for j in range(2):
                    dve.wait_ge(*act_done("gexp", j))
                    d(stt(tile(GQ0 + j), tile(GQ0 + j), 0.125, tile(35 + j), ALU.mult, ALU.mult))
                    d(ve.tensor_tensor(tile(33 + j), tile(33 + j), tile(GK0 + j), ALU.mult), "kdec", j)
                    d(ve.tensor_tensor(tile(GK0 + j), tile(GK0 + j), tile(29 + j), ALU.mult), "kn", j)
                for j in range(2):
                    dve.wait_ge(*pe_done("kv", j))
                    for c in range(NCH - 1):
                        kv = PS[4 + 2 * j + c // 4][:, col(c % 4)]
                        last = ("states",) if j == 1 and c == NCH - 2 else ()
                        if c == 0:
                            d(ve.tensor_copy(gla_state(j, 1), kv))
                        else:
                            d(stt(gla_state(j, c + 1), gla_state(j, c), tile(35 + j)[:, c * CH + CH - 1:c * CH + CH], kv,
                                  ALU.mult, ALU.add), *last)
                for h in range(4):
                    dve.wait_ge(*pe_done("gatt", h))
                    dve.wait_ge(*act_done("kdT", 1))
                    d(stt(by_tt(tile(GATT[h])), by_tt(PS[h][:]), 3e38, mask4("incl"), ALU.min, ALU.mult), "gatt", h)
                dve.wait_ge(*act_done("ggate"))
                head_norms("gla", 4, Y_MIX[0], v("glan"), GG0)

            def delta_rule():
                for first in range(0, 12, 2):
                    for t in (first, first + 1):
                        d(ve.tensor_scalar(tile(t), tile(DQ0 + t), v("gdnconv", 36 + t), None, ALU.mult), pair=True)
                    for lag in range(1, 4):
                        for t in (first, first + 1):
                            x, y = tile(DQ0 + t), tile(t)
                            d(stt(y[:, lag:T], x[:, 0:T - lag], v("gdnconv", 12 * (3 - lag) + t), y[:, lag:T],
                                  ALU.mult, ALU.add), *(("dconv", t) if lag == 3 else ()), pair=True)
                d(ve.memset(tile(22), 0.0), "rows0")
                g, e = slice(DA_ROW, DA_ROW + 4), slice(ED_ROW, ED_ROW + 4)
                dve.wait_ge(*act_done("dsp"))
                d(stt(tile(SM0)[g], tile(SM0)[g], 0.0, tile(21)[g], ALU.max, ALU.add))
                d(ve.tensor_scalar(tile(SM0)[g], tile(SM0)[g], STAT[g, 0, 0:1], -1.0, ALU.mult, ALU.mult))
                d(ve.tensor_tensor_scan(tile(22)[g], cst("reset")[g], tile(SM0)[g], 0.0, ALU.mult, ALU.add))
                b = by_chunk(tile(22))[g]
                dve.wait_ge(*act_done("beta"))
                d(ve.tensor_tensor(by_chunk(tile(22))[e], b[:, :, CH - 1:CH].broadcast_to([4, NCH, CH]), b,
                                   ALU.subtract), "gc")
                for t in range(8):
                    dve.wait_ge(*act_done("l2sd", t))
                    d(ve.reciprocal(tile(13 + t), tile(13 + t)))
                    d(stt(tile(t), tile(t), 128 ** -0.5 if t < 4 else 1.0, tile(13 + t), ALU.mult, ALU.mult), "l2n", t)
                dve.wait_ge(*act_done("cols"))
                for tt in range(TT):
                    cols = tile(23)[:, col(tt)]
                    d(ve.tensor_tensor(STAT[:, 1, 4 * tt:4 * tt + 4], cols[:, EG_ROW:EG_ROW + 4],
                                       cols[:, DB_ROW:DB_ROW + 4], ALU.mult), *(("colbe",) if tt == TT - 1 else ()))
                for h in range(4):
                    dve.wait_ge(*act_done("egb", h))
                    for tt in range(TT):
                        c = tt * P + DA_ROW + h
                        d(ve.tensor_scalar(tile(29 + h)[:, col(tt)], PS[h][:, col(tt)], tile(23)[:, c:c + 1], 0.0,
                                           ALU.subtract, ALU.min), *(("ddec", h) if tt == TT - 1 else ()), chain=False)
                for h in range(4):
                    d(ve.tensor_tensor(tile(37 + h), tile(4 + h), PS[4 + h][:], ALU.mult), "kb", h)
                    dve.wait_ge(*act_done("ddec", h))
                    d(ve.tensor_tensor(by_tt(tile(29 + h)), by_tt(tile(29 + h)), mask4("incl"), ALU.mult))
                    d(ve.tensor_tensor(tile(13 + h), tile(h), tile(33 + h), ALU.mult))
                for h in range(4):
                    dve.wait_ge(*pe_done("datt", h))
                    d(ve.tensor_tensor(tile(h), PS[h][:], tile(29 + h), ALU.mult))
                    d(ve.tensor_tensor(tile(17 + h), PS[4 + h][:], tile(29 + h), ALU.mult))
                    d(ve.tensor_tensor(by_tt(tile(17 + h)), by_tt(tile(17 + h)), mask4("strict"), ALU.mult), "dLT", h)
                dve.wait_ge(*pe_done("dtok", 3))
                dve.wait_ge(*act_done("dtok", 3))
                invert(("gdn", 0))
                dve.wait_ge(*act_done("du", 3))
                for c in range(NCH):
                    r, tt = slice(CH * (c % 2), CH * (c % 2) + CH), c // 2
                    if c == 0:
                        d(ve.tensor_copy(tile(8)[r], tile(17)[r]), "dv", c)
                    else:
                        dve.wait_ge(*pe_done("dws", c))
                        d(ve.tensor_tensor(tile(8 + tt)[r], tile(17 + tt)[r], PS[0][r, :], ALU.subtract), "dv", c)
                    if c < NCH - 1:
                        dve.wait_ge(*pe_done("dupd", c))
                        if c == 0:
                            d(ve.tensor_copy(STATE[:], PS[1][:]), "dstate", c)
                        else:
                            for h in range(4):
                                d(stt(STATE[:, col(h)], STATE[:, col(h)], tile(33 + h)[:, c * CH + CH - 1:c * CH + CH],
                                      PS[1][:, col(h)], ALU.mult, ALU.add), *(("dstate", c) if h == 3 else ()),
                                  chain=(h == 3))
                head_norms("gdn", 4, Y_MIX[0][4:], v("gdnn"), DZ0)

            def lru():
                dve.wait_ge(tile_copied, COPIED["mix1"] + N_ODD)
                for first in (0, 2):
                    for j in (first, first + 1):
                        d(ve.tensor_scalar(tile(22 + j), tile(LX0 + j), v("lconv", 12 + j), v("lconvb", j),
                                           ALU.mult, ALU.add), pair=True)
                    for lag in range(1, 4):
                        for j in (first, first + 1):
                            x, y = tile(LX0 + j), tile(22 + j)
                            d(stt(y[:, lag:T], x[:, 0:T - lag], v("lconv", 4 * (3 - lag) + j), y[:, lag:T],
                                  ALU.mult, ALU.add), *(("lconv", j) if lag == 3 else ()), pair=True)
                dve.wait_ge(*act_done("lam"))
                z, s, s2, acc = (LRUV[:, 4 * i:4 * i + 4] for i in range(4))
                d(ve.tensor_scalar(s, z, 2.0, None, ALU.add))
                d(ve.reciprocal(s, s))
                d(ve.tensor_tensor(s, s, z, ALU.mult))
                d(ve.tensor_tensor(s2, s, s, ALU.mult))
                d(ve.tensor_scalar(acc, s2, 1 / 17, 1 / 15, ALU.mult, ALU.add))
                for n in (13, 11, 9, 7, 5, 3, 1):
                    d(ve.tensor_tensor(acc, acc, s2, ALU.mult))
                    d(ve.tensor_scalar(acc, acc, 1 / n, None, ALU.add))
                d(ve.tensor_tensor(acc, acc, s, ALU.mult))
                d(ve.tensor_scalar(z, v4("lam"), -1.0, 0.0, ALU.mult, ALU.max))
                d(stt(z, acc, 2.0, z, ALU.mult, ALU.add))
                d(ve.tensor_scalar(LRUV[:, 8:12], z, -8.0, None, ALU.mult))
                d(ve.tensor_scalar(LRUV[:, 12:16], z, 8.0, None, ALU.mult), "lam")
                for j in range(4):
                    g, y = tile(14 + j), tile(LY0 + j)
                    d(ve.tensor_tensor(g, y, y, ALU.mult))
                    d(ve.tensor_scalar(g, g, 0.044715, 1.0, ALU.mult, ALU.add))
                    d(ve.tensor_tensor(g, g, y, ALU.mult), "gelu0", j)
                for j in range(4):
                    dve.wait_ge(*act_done("ltanh", j))
                    m = tile(38 + j)
                    d(ve.tensor_scalar(m, tile(26 + j), 1.0, None, ALU.add))
                    d(ve.reciprocal(m, m))
                    d(stt(m, tile(26 + j), 2.0, m, ALU.mult, ALU.mult))
                    d(ve.tensor_scalar(m, m, 0.0, None, ALU.max), "lmult", j)
                for j in range(4):
                    dve.wait_ge(*act_done("gelu", j))
                    d(stt(tile(14 + j), tile(14 + j), 1.0, tile(LY0 + j), ALU.add, ALU.mult))
                    dve.wait_ge(*act_done("lmult", j))
                    d(ve.tensor_tensor(tile(38 + j), tile(38 + j), tile(30 + j), ALU.mult))
                    d(ve.tensor_tensor(tile(38 + j), tile(38 + j), tile(22 + j), ALU.mult))
                    d(ve.tensor_tensor_scan(tile(30 + j), tile(34 + j), tile(38 + j), 0.0, ALU.mult, ALU.add))
                    d(stt(tile(Y_MIX[1][j]), tile(30 + j), 0.5, tile(14 + j), ALU.mult, ALU.mult),
                      "t", "mixout1", j)

            def rwkv():
                n = LX0
                d(ve.tensor_tensor(BIG[:, 22:22 + n, 1:T], BIG[:, 0:n, 0:T - 1], BIG[:, 0:n, 1:T], ALU.subtract),
                  chain=False)
                d(ve.tensor_scalar(BIG[:, 22:22 + n, 0:1], BIG[:, 0:n, 0:1], -1.0, None, ALU.mult))
                for t in (WA0, GL0, *range(WA0)):
                    d(stt(tile(t), tile(22 + t), v("mu", t), tile(t), ALU.mult, ALU.add), "shift", t)
                for j in range(4):
                    d(ve.tensor_scalar(tile(36 + j), tile(RK0 + j), v("kk", j), None, ALU.mult), "kk", j)
                for j in range(4):
                    dve.wait_ge(*act_done("rgate", j))
                    dve.wait_ge(*act_done("kksd", j))
                    d(ve.reciprocal(tile(40 + j), tile(40 + j)))
                    d(ve.tensor_tensor(tile(36 + j), tile(36 + j), tile(40 + j), ALU.mult))
                    d(ve.tensor_scalar(tile(40 + j), tile(28 + j), 1.0, v("ka", j), ALU.subtract, ALU.mult))
                    d(stt(tile(RK0 + j), tile(40 + j), 1.0, tile(RK0 + j), ALU.add, ALU.mult))
                    d(stt(tile(14 + j), tile(R0 + j), v("rk", j), tile(RK0 + j), ALU.mult, ALU.mult), "bonus0", j)
                for j in range(4):
                    dve.wait_ge(*pe_done("bonus", j))
                    d(ve.tensor_tensor(tile(14 + j), PS[4 + j][:], tile(RV0 + j), ALU.mult))
                for j in range(4):
                    d(ve.tensor_tensor_scan(tile(40 + j), cst("reset"), tile(24 + j), 0.0, ALU.mult, ALU.add))
                    b = by_chunk(tile(40 + j))
                    d(ve.tensor_tensor(tile(24 + j), tile(40 + j), tile(24 + j), ALU.subtract))
                    d(ve.tensor_tensor(by_chunk(tile(18 + j)), b[:, :, CH - 1:CH].broadcast_to([P, NCH, CH]), b,
                                       ALU.subtract))
                    d(ve.tensor_tensor(tile(28 + j), tile(28 + j), tile(36 + j), ALU.mult), "rcum", j)
                for j in range(4):
                    dve.wait_ge(*act_done("rexp", j))
                    d(stt(tile(24 + j), tile(36 + j), -1.0, tile(24 + j), ALU.mult, ALU.mult))
                    d(ve.tensor_tensor(tile(j), tile(j), tile(32 + j), ALU.mult))
                    d(ve.tensor_copy(STAT[:, 2, 8 * j:8 * j + 8], by_chunk(tile(32 + j))[:, :, CH - 1]))
                    d(ve.tensor_tensor(tile(36 + j), tile(28 + j), tile(40 + j), ALU.mult))
                    d(ve.tensor_tensor(tile(28 + j), tile(28 + j), tile(18 + j), ALU.mult))
                    d(ve.tensor_tensor(tile(18 + j), tile(18 + j), tile(4 + j), ALU.mult))
                    d(ve.tensor_tensor(tile(4 + j), tile(4 + j), tile(40 + j), ALU.mult),
                      *(("rprep",) if j == 3 else ()))
                for tt in range(TT):
                    m = ("rwkv", tt)
                    dve.wait_ge(*pe_done("rmat", tt))
                    def masked(o, bank, name, sign=None):
                        for g in range(2):
                            o4 = o[:, 256 * g:256 * g + 256].rearrange("p (j c) -> p j c", j=4)
                            x4 = PS[bank + g][:, 0:256].rearrange("p (j c) -> p j c", j=4)
                            if sign is None:
                                ins = ve.tensor_tensor(o4, x4, mask_chunks(name), ALU.mult)
                            else:
                                ins = stt(o4, x4, sign, mask_chunks(name), ALU.mult, ALU.mult)
                            if g == 0:
                                d(ins, chain=False)
                        return ins

                    d(masked(tile(33), 4, "strict", -1.0), chain=False)
                    d(masked(RT["aak"], 6, "strict"), "rmat", tt)
                    dve.wait_ge(*pe_done("rz", tt))
                    invert(m)
                    dve.wait_ge(*pe_done("rout", tt))
                    d(masked(RT["rb"], 4, "incl"), chain=False)
                    d(masked(RT["rk"], 6, "incl"), "rout", tt)
                    dve.wait_ge(*act_done("ru", tt))
                    for c in (2 * tt, 2 * tt + 1):
                        r = slice(CH * (c % 2), CH * (c % 2) + CH)
                        if c:
                            dve.wait_ge(*pe_done("rws", c))
                            for g in range(2):
                                z = RT["z"][r, 256 * g:256 * g + 256]
                                d(ve.tensor_tensor(z, z, PS[3 + g][r, 0:256], ALU.add),
                                  *(("ruc", c) if g else ()), chain=bool(g))
                        else:
                            d(ve.memset(STAT[:, 3, 0:1], 0.0), "ruc", c)
                        if c < NCH - 1:
                            dve.wait_ge(*pe_done("rupd", c))
                            if c == 0:
                                d(ve.tensor_copy(STATE[:, 0:256], PS[1][:, 0:256]), "rstate", c)
                            else:
                                for j in range(4):
                                    d(stt(STATE[:, col(j, 64)], STATE[:, col(j, 64)],
                                          STAT[:, 2, 8 * j + c:8 * j + c + 1], PS[1][:, col(j, 64)],
                                          ALU.mult, ALU.add), *(("rstate", c) if j == 3 else ()), chain=(j == 3))
                for j in range(4):
                    dve.wait_ge(*pe_done("gmean", j))
                    dve.wait_ge(*act_done("ry", TT - 1))
                    d(ve.tensor_tensor(tile(j), tile(j), PS[j][:], ALU.subtract), "gcentred", j, chain=False)
                for j in range(4):
                    dve.wait_ge(*act_done("gsd", j))
                    d(ve.reciprocal(tile(22 + j), tile(22 + j)))
                    d(stt(tile(j), tile(j), v("lnw", j), tile(22 + j), ALU.mult, ALU.mult))
                    d(stt(tile(j), tile(j), v("lnbb", j), tile(14 + j), ALU.add, ALU.add))
                    dve.wait_ge(*pe_done("gout", j))
                    d(ve.tensor_tensor(tile(j), tile(j), PS[j][:], ALU.mult), "t", "mixout1", 4 + j)

            modulation()
            for u in range(SPLIT):
                low(u)
            for l in range(DEPTH):
                layer_norm(("ln", l), l, True)
                lows(f"first{l}")
                rope_and_attention(l)
                short_conv(l)
                for j in range(2):
                    dve.wait_ge(*pe_done("four", l, j))
                    d(ve.tensor_tensor(tile(Y_FIRST[6 + j]), PS[4 + j][:], tile(GF0 + j), ALU.mult), "four", l, j)
                split_tiles(f"firstout{l}", lambda k: tile(Y_FIRST[k]))
                lows(f"firstout{l}")
                residual(l)
                layer_norm(("pln", l), l, False)
            for i in range(DEPTH):
                pre_norm(f"{i}0", 6 * i)
                ffn(f"{i}0")
                post_norm(f"{i}0", 6 * i + 1, 0.5)
                pre_norm(f"mix{i}", 6 * i + 2)
                lows(f"mix{i}")
                if i % 2 == 0:
                    linear_attention()
                    delta_rule()
                else:
                    lru()
                    rwkv()
                split_tiles(f"mixout{i}", lambda k: tile(Y_MIX[i][k]))
                lows(f"mixout{i}")
                dve.wait_ge(tile_copied, COPIED[f"mixout{i}"] + KT)
                post_norm(f"mix{i}", 6 * i + 3, 1.0)
                pre_norm(f"{i}1", 6 * i + 4)
                ffn(f"{i}1")
                post_norm(f"{i}1", 6 * i + 5, 0.5)
            d(ve.memset(STAT[:, 3, 0:1], 0.0), "x", "end")

    return seen


def _units(w, k_tiles=KT):
    k, n = w.shape
    return w.reshape(k_tiles, P, n // P, P).transpose(2, 1, 0, 3).reshape(n // P, P, k_tiles * P)


def _columns(a):
    return a.reshape(-1, P).T


def _heads_order():
    return np.concatenate([np.arange(h * 64, h * 64 + 64) for t in range(4) for h in (t, 4 + t)])


def _weights(a):
    heads, k_units, down0, down1 = _heads_order(), [], [], []
    for l in range(DEPTH):
        w = a["w_in"][l]
        k_units.append(_units(np.concatenate([w[:, heads], w[:, 512:768], w[:, 768 + heads], w[:, 1280:]], 1)))
        w = a["w_out"][l]
        k_units.append(_units(np.concatenate([w[heads], w[512:]], 0)))

    def ffn(i, j):
        at = 0
        for half, down in zip(HALVES, (down0, down1)):
            f = slice(at * P, (at + half) * P)
            g, u = _units(a["ffn_w_gate_2"][i, j][:, f]), _units(a["ffn_w_up_2"][i, j][:, f])
            k_units.append(np.stack([g, u], 1).reshape(2 * half, P, UNIT))
            w = a["ffn_w_down_2"][i, j][f].reshape(2, half // 2, P, KT, P)
            down.append(w.transpose(3, 0, 2, 1, 4).reshape(2 * KT, P, half // 2 * P))
            at += half

    for i in range(DEPTH):
        ffn(i, 0)
        if i % 2 == 0:
            w = a["even_w_in_2"][i // 2]
            small = np.zeros((D, P), w.dtype)
            small[:, GLR_ROW:GLR_ROW + 16] = w[:, 1536:1552]
            small[:, DA_ROW:DA_ROW + 4] = w[:, 3600:3604]
            small[:, DB_ROW:DB_ROW + 4] = w[:, 3604:3608]
            k_units.append(_units(np.concatenate([w[:, :1536], small, w[:, 1552:3600]], 1)))
            k_units.append(_units(a["even_w_out_2"][i // 2]))
        else:
            k_units.append(_units(a["odd_w_in_2"][i // 2]))
            w = a["odd_w_out_2"][i // 2]
            k_units.append(_units(np.concatenate([w[512:], w[:512]], 0)))
        ffn(i, 1)
    k_units.append(k_units[0][:SPLIT])
    return np.concatenate(k_units), np.concatenate(down0), np.concatenate(down1)


def _vectors(a):
    dt = a["x"].dtype
    out = np.zeros((P, NV), dt)

    def put(name, x, rows=slice(None)):
        out[rows, VCOL[name]:VCOL[name] + x.shape[1]] = x

    put("c", _columns(a["c"][0]))
    put("bada", np.concatenate([_columns(b) for b in a["b_ada"]], 1))
    put("qg", np.concatenate([a["q_gain"], a["q_gain"]], 1).T)
    put("kg", np.concatenate([a["k_gain"], a["k_gain"]], 1).T)
    put("cw", np.concatenate([_columns(w) for w in a["conv_w"]], 1))
    put("lng", np.concatenate([_columns(w) for w in a["ln_g"]], 1))
    put("lnb", np.concatenate([_columns(w) for w in a["ln_b"]], 1))
    put("nw", _columns(a["norm_w_2"]))
    put("lorab", _columns(a["gla_lora_b_2"]))
    put("glan", _columns(a["gla_norm_2"]))
    put("gdnconv", _columns(a["gdn_conv_2"]))
    put("alog", a["gdn_a_log_2"].T, slice(DA_ROW, DA_ROW + 4))
    put("dtb", a["gdn_dt_bias_2"].T, slice(DA_ROW, DA_ROW + 4))
    put("gdnn", _columns(a["gdn_norm_2"]))
    for name, key in (("mu", "rwkv_mu"), ("w0", "rwkv_w0"), ("a0", "rwkv_a0"), ("kk", "rwkv_k_k"), ("ka", "rwkv_k_a"),
                      ("rk", "rwkv_r_k"), ("lnw", "rwkv_ln_w"), ("lnbb", "rwkv_ln_b"), ("lconv", "lru_conv_w"),
                      ("lconvb", "lru_conv_b"), ("lba", "lru_ba"), ("lbx", "lru_bx"), ("lam", "lru_lambda")):
        put(name, _columns(a[key + "_2"]))
    for name, value in (("eps6", 1e-6), ("eps5", 1e-5), ("epsg", 64e-5), ("one", 1.0)):
        out[:, VCOL[name]] = value
    return out


def _small_weights(a):
    dt = a["x"].dtype
    out = np.zeros((P, NS), dt)
    for l in range(DEPTH):
        for g in range(4):
            j, s = g // 2, 64 * (g % 2)
            c = SCOL["fmix"] + l * 2 * P + j * P + s
            out[s:s + 64, c:c + 64] = a["f_mix"][l, g]
    out[0:16, SCOL["lora"]:SCOL["lora"] + 2 * P] = a["gla_lora_w2_2"][0]
    out[0:64, SCOL["wa2"]:SCOL["wa2"] + 4 * P] = a["rwkv_w2_2"][0]
    out[64:128, SCOL["wa2"]:SCOL["wa2"] + 4 * P] = a["rwkv_a2_2"][0]
    out[:, SCOL["g2"]:SCOL["g2"] + 4 * P] = a["rwkv_g2_2"][0]
    for b in range(8):
        j, s = b // 2, 64 * (b % 2)
        for name, key in (("lwa", "lru_wa_2"), ("lwx", "lru_wx_2")):
            c = SCOL[name] + j * P + s
            out[s:s + 64, c:c + 64] = a[key][0, b]
    return out


def _constants():
    f32 = np.float32
    out = np.zeros((P, NC), f32)

    def put(name, x):
        c, n = CCOL[name]
        out[:, c:c + n] = x

    half = 32
    inv_freq = (f32(1.0) / (f32(10000.0) ** (np.arange(0, half, 2, dtype=f32) / f32(half)))).astype(f32)
    row, column = np.arange(T) // 64, np.arange(T) % 64
    p = np.arange(P)
    position = np.where((p % 64 < half)[:, None], row, column).astype(f32)
    angle = position * inv_freq[p % 16][:, None]
    put("cos", np.cos(angle))
    put("sin", np.sin(angle))
    perm = np.zeros((P, P), f32)
    first = p % 32 < 16
    perm[p[first] + 16, p[first]] = -1.0
    perm[p[~first] - 16, p[~first]] = 1.0
    put("perm", perm)
    put("reset", (np.arange(T) % CH != 0).astype(f32))
    key, query = p[:, None], p[None, :]
    same = key // CH == query // CH
    put("ident", np.eye(P))
    put("incl", same & (query >= key))
    put("strict", same & (query > key))
    for b in range(LEVELS):
        w = 1 << b
        put(f"lev{b}", (key // (2 * w) == query // (2 * w)) & (key // w % 2 == 0) & (query // w % 2 == 1))
    for name in ("ident", "incl", "strict", *[f"lev{b}" for b in range(LEVELS)]):
        c = CCOL[name][0]
        block = out[0:CH, c:c + CH]
        put(name + "c", np.concatenate([block, block], 0))
    put("onesD", 1.0 / D)
    put("ones128", 1.0 / P)
    put("ones1", 1.0)
    put("blk1", (key // 64 == query // 64))
    put("blk64", (key // 64 == query // 64) / 64.0)
    for h in range(4):
        c = CCOL["sel"][0] + h * P
        out[DA_ROW + h, c:c + P] = 1.0
        out[DB_ROW + h, c:c + P] = 1.0
    d = np.arange(64)
    turn = 2 * np.pi * ((d[:, None] * d[None, :]) % 64) / 64
    for name, m in (("c64", np.cos(turn)), ("s64", np.sin(turn))):
        put(name, np.kron(np.eye(2), m))
    t = np.arange(T)
    turn = 2 * np.pi * ((t[:, None] * t[None, :]) % T) / T
    scale = 1.0 / np.sqrt(T * 64.0)
    dft = np.stack([np.cos(turn) * scale, -np.sin(turn) * scale])
    dft = dft.reshape(2, TT, P, T).transpose(2, 0, 1, 3).reshape(P, 2 * TT, T)
    return out, dft.astype(f32)


def kernel(**inputs):
    import numpy as _np
    import concourse.bacc as _bacc
    from concourse import mybir as _mybir
    from concourse.bass_utils import run_bass_kernel_spmd as _run

    a = {name: _np.asarray(x) for name, x in inputs.items()}
    w_k, w_d0, w_d1 = _weights(a)
    w_ada = np.stack([w[:, q * D:q * D + D].reshape(KT, P, 2, T).transpose(1, 0, 2, 3).reshape(P, 16, T)
                      for w in a["w_ada"] for q in range(3)])
    constants, dft = _constants()
    x = a["x"][0].T.reshape(KT, P, T).transpose(1, 0, 2)
    arrays = {"x_in": x, "w_k": w_k, "w_d0": w_d0, "w_d1": w_d1, "w_ada": w_ada, "vec_in": _vectors(a), "cst_in": constants,
              "small_in": _small_weights(a), "dft_in": dft}
    arrays = {name: _np.ascontiguousarray(v) for name, v in arrays.items()}

    def program(known):
        nc = _bacc.Bacc("TRN2", target_bir_lowering=False, num_devices=1)
        args = [nc.dram_tensor(name, v.shape, _mybir.dt.from_np(v.dtype), kind="ExternalInput").ap()
                for name, v in arrays.items()]
        out = nc.dram_tensor("out_0_dram", (P, KT, T), _mybir.dt.from_np(_np.dtype("float32")),
                             kind="ExternalOutput").ap()
        return nc, write_program(nc, known, *args, out)

    _, known = program({})
    nc, _ = program(known)
    r = _run(nc, [arrays], core_ids=[0])
    y = r.results[0]["out_0_dram"]
    return y.transpose(1, 0, 2).reshape(D, T).T.reshape(1, T, D)
```
